# Optimizing a Trainium2 kernel written in Bass

```python
import jax, jax.numpy as jnp
from jax import lax
import numpy as np

D_MODEL = 1024
BATCH = 1
SEQ = 1024
DEPTH = 1

D_MIX = D_MODEL
SB_HEADS = 8
SB_HEAD_DIM = 64
SB_WIDTH = SB_HEADS * SB_HEAD_DIM
GLA_HEADS = 4
GLA_DK = 64
GLA_DV = 128
GLA_KW = GLA_HEADS * GLA_DK
GLA_VW = GLA_HEADS * GLA_DV
GLA_GATE_RANK = 16
GLA_GATE_TAU = 16.0
GLA_CHUNK = 64
Q_BLOCK = 128
D_IN = 3 * SB_WIDTH + 2 * GLA_KW + 2 * GLA_VW + GLA_GATE_RANK
N_GROUPS = 4
EXPERTS_PER_GROUP = 8
N_EXPERTS = N_GROUPS * EXPERTS_PER_GROUP
TOP_K = 2
D_FF_EXPERT = 512
MOE_BLOCK = 128
RMS_EPS = 1e-6

kernel_name = "hymba_stickbreak_gla_hiermoe"

def rmsnorm(x, g):
    xf = x.astype(jnp.float32)
    inv = lax.rsqrt(jnp.mean(xf * xf, axis=-1, keepdims=True) + RMS_EPS)
    return (xf * inv).astype(x.dtype) * g

def stick_breaking_attention(q, k, v):
    B, H, S, Dh = q.shape
    nb = S // Q_BLOCK
    scale = Dh ** -0.5
    key_pos = jnp.arange(S)
    qb = q.reshape(B, H, nb, Q_BLOCK, Dh).transpose(2, 0, 1, 3, 4)

    def block(args):
        i, q_i = args
        q_pos = i * Q_BLOCK + jnp.arange(Q_BLOCK)
        z = jnp.einsum('bhqd,bhkd->bhqk', q_i, k).astype(jnp.float32) * scale
        mask = key_pos[None, :] < q_pos[:, None]
        log_beta = jax.nn.log_sigmoid(z)
        log_one_minus = jnp.where(mask, jax.nn.log_sigmoid(-z), 0.0)
        later = lax.cumsum(log_one_minus, axis=3, reverse=True) - log_one_minus
        weights = jnp.where(mask, jnp.exp(log_beta + later), 0.0)
        return jnp.einsum('bhqk,bhkd->bhqd', weights.astype(v.dtype), v)

    out = lax.map(block, (jnp.arange(nb), qb))
    return out.transpose(1, 2, 0, 3, 4).reshape(B, H, S, Dh)

def gla_chunked(q, k, v, log_a):
    B, H, S, Dk = q.shape
    Dv = v.shape[-1]
    nc = S // GLA_CHUNK

    def to_chunks(t):
        return t.astype(jnp.float32).reshape(B, H, nc, GLA_CHUNK, t.shape[-1]).transpose(2, 0, 1, 3, 4)

    causal = jnp.tril(jnp.ones((GLA_CHUNK, GLA_CHUNK), dtype=bool))

    def step(state, inp):
        q_c, k_c, v_c, g_c = inp
        b = jnp.cumsum(g_c, axis=2)
        o_inter = jnp.einsum('bhtk,bhkv->bhtv', q_c * jnp.exp(b), state)
        diff = b[:, :, :, None, :] - b[:, :, None, :, :]
        decay = jnp.where(causal[:, :, None], jnp.exp(jnp.minimum(diff, 0.0)), 0.0)
        scores = jnp.einsum('bhtk,bhsk,bhtsk->bhts', q_c, k_c, decay)
        o_intra = jnp.einsum('bhts,bhsv->bhtv', scores, v_c)
        b_last = b[:, :, -1:, :]
        k_dec = k_c * jnp.exp(b_last - b)
        state = jnp.exp(b_last)[:, :, 0, :, None] * state + jnp.einsum('bhsk,bhsv->bhkv', k_dec, v_c)
        return state, o_inter + o_intra

    state0 = jnp.zeros((B, H, Dk, Dv), jnp.float32)
    _, out = lax.scan(step, state0, (to_chunks(q), to_chunks(k), to_chunks(v), to_chunks(log_a)))
    return out.transpose(1, 2, 0, 3, 4).reshape(B, H, S, Dv).astype(v.dtype)

def hybrid_mixer(h, w_in, gla_gate_w2, gla_gate_b, gla_norm_g, w_out):
    B, S, _ = h.shape
    proj = h @ w_in
    sizes = (SB_WIDTH, SB_WIDTH, SB_WIDTH, GLA_KW, GLA_KW, GLA_VW, GLA_VW, GLA_GATE_RANK)
    points = [int(p) for p in np.cumsum(sizes)[:-1]]
    sb_q, sb_k, sb_v, g_q, g_k, g_v, g_r, g_lr = jnp.split(proj, points, axis=-1)

    def heads(t, n):
        return t.reshape(B, S, n, -1).transpose(0, 2, 1, 3)

    o_sb = stick_breaking_attention(heads(sb_q, SB_HEADS), heads(sb_k, SB_HEADS), heads(sb_v, SB_HEADS))
    o_sb = o_sb.transpose(0, 2, 1, 3).reshape(B, S, SB_WIDTH)

    log_a = jax.nn.log_sigmoid((g_lr @ gla_gate_w2 + gla_gate_b).astype(jnp.float32)) / GLA_GATE_TAU
    o_gla = gla_chunked(heads(g_q * (GLA_DK ** -0.5), GLA_HEADS), heads(g_k, GLA_HEADS),
                        heads(g_v, GLA_HEADS), heads(log_a, GLA_HEADS))
    o_gla = rmsnorm(o_gla.transpose(0, 2, 1, 3), gla_norm_g.reshape(GLA_HEADS, GLA_DV))
    o_gla = o_gla.reshape(B, S, GLA_VW) * jax.nn.silu(g_r)

    return jnp.concatenate([o_sb, o_gla], axis=-1) @ w_out

def hierarchical_moe(h, w_group, b_group, w_expert, b_expert, exp_w_gate, exp_w_up, exp_w_down):
    B, S, D = h.shape
    T = B * S
    xt = h.reshape(T, D)
    tok = jnp.arange(T)
    group_logits = (xt @ w_group).astype(jnp.float32) + b_group
    group_prob = jax.nn.softmax(group_logits, axis=-1)
    g_idx = jnp.argmax(group_logits, axis=-1)
    g_p = group_prob[tok, g_idx][:, None]
    exp_logits = ((xt @ w_expert).astype(jnp.float32) + b_expert).reshape(T, N_GROUPS, EXPERTS_PER_GROUP)
    sel = exp_logits[tok, g_idx]
    top_w, top_i = lax.top_k(jax.nn.softmax(sel, axis=-1), TOP_K)
    top_w = top_w / jnp.sum(top_w, axis=-1, keepdims=True)
    gate = g_p * top_w
    expert_id = g_idx[:, None] * EXPERTS_PER_GROUP + top_i

    N = T * TOP_K
    e_flat = expert_id.reshape(N)
    tok_flat = jnp.repeat(jnp.arange(T, dtype=jnp.int32), TOP_K)
    gate_flat = gate.reshape(N)
    order = jnp.argsort(e_flat)
    e_sorted = e_flat[order]
    counts = jnp.bincount(e_flat, length=N_EXPERTS)
    starts = jnp.cumsum(counts) - counts
    padded = (counts + MOE_BLOCK - 1) // MOE_BLOCK * MOE_BLOCK
    padded_ends = jnp.cumsum(padded)
    padded_starts = padded_ends - padded
    dest = padded_starts[e_sorted] + (jnp.arange(N) - starts[e_sorted])
    n_slots = N + N_EXPERTS * MOE_BLOCK
    n_blocks = n_slots // MOE_BLOCK
    slot_tok = jnp.full((n_slots,), T, jnp.int32).at[dest].set(tok_flat[order])
    slot_gate = jnp.zeros((n_slots,), jnp.float32).at[dest].set(gate_flat[order])
    block_start = jnp.arange(n_blocks) * MOE_BLOCK
    block_expert = jnp.minimum(jnp.searchsorted(padded_ends, block_start, side='right'), N_EXPERTS - 1)

    x_pad = jnp.concatenate([xt, jnp.zeros((1, D), xt.dtype)], axis=0)
    xb = x_pad[slot_tok].reshape(n_blocks, MOE_BLOCK, D)

    def expert_block(args):
        e, x_blk = args
        hidden = jax.nn.silu(x_blk @ exp_w_gate[e]) * (x_blk @ exp_w_up[e])
        return hidden @ exp_w_down[e]

    yb = lax.map(expert_block, (block_expert, xb))
    y = yb.reshape(n_slots, D) * slot_gate[:, None].astype(yb.dtype)
    out = jnp.zeros((T + 1, D), y.dtype).at[slot_tok].add(y)[:T]
    return out.reshape(B, S, D)

def setup_inputs(seed: int = 0) -> dict:
    key = jax.random.key(seed)
    ks = jax.random.split(key, 16)
    f32 = jnp.float32
    nrm = lambda k, shape, s: jax.random.normal(k, shape, f32) * s
    return {
        "x": nrm(ks[0], (BATCH, SEQ, D_MODEL), 1.0),
        "ln1_g": 1.0 + nrm(ks[1], (DEPTH, D_MODEL), 0.02),
        "w_in": nrm(ks[2], (DEPTH, D_MODEL, D_IN), D_MODEL ** -0.5),
        "gla_gate_w2": nrm(ks[3], (DEPTH, GLA_GATE_RANK, GLA_KW), GLA_GATE_RANK ** -0.5),
        "gla_gate_b": nrm(ks[4], (DEPTH, GLA_KW), 0.1),
        "gla_norm_g": 1.0 + nrm(ks[5], (DEPTH, GLA_VW), 0.02),
        "w_out": nrm(ks[6], (DEPTH, D_MIX, D_MODEL), D_MIX ** -0.5),
        "ln2_g": 1.0 + nrm(ks[7], (DEPTH, D_MODEL), 0.02),
        "w_group": nrm(ks[8], (DEPTH, D_MODEL, N_GROUPS), D_MODEL ** -0.5),
        "b_group": nrm(ks[9], (DEPTH, N_GROUPS), 0.01),
        "w_expert": nrm(ks[10], (DEPTH, D_MODEL, N_EXPERTS), D_MODEL ** -0.5),
        "b_expert": nrm(ks[11], (DEPTH, N_EXPERTS), 0.01),
        "exp_w_gate": nrm(ks[12], (DEPTH, N_EXPERTS, D_MODEL, D_FF_EXPERT), D_MODEL ** -0.5),
        "exp_w_up": nrm(ks[13], (DEPTH, N_EXPERTS, D_MODEL, D_FF_EXPERT), D_MODEL ** -0.5),
        "exp_w_down": nrm(ks[14], (DEPTH, N_EXPERTS, D_FF_EXPERT, D_MODEL), D_FF_EXPERT ** -0.5),
        "ln_f_g": 1.0 + nrm(ks[15], (D_MODEL,), 0.02),
    }

def reference(x, ln1_g, w_in, gla_gate_w2, gla_gate_b, gla_norm_g, w_out, ln2_g,
              w_group, b_group, w_expert, b_expert, exp_w_gate, exp_w_up, exp_w_down, ln_f_g):
    for l in range(DEPTH):
        h = rmsnorm(x, ln1_g[l])
        x = x + hybrid_mixer(h, w_in[l], gla_gate_w2[l], gla_gate_b[l], gla_norm_g[l], w_out[l])
        h = rmsnorm(x, ln2_g[l])
        x = x + hierarchical_moe(h, w_group[l], b_group[l], w_expert[l], b_expert[l],
                                 exp_w_gate[l], exp_w_up[l], exp_w_down[l])
    return rmsnorm(x, ln_f_g)


_drawn_inputs = setup_inputs


def setup_inputs(seed=0):
    import zlib

    import numpy as np

    out = dict(_drawn_inputs(seed))
    spreads = {}
    factors = {'gla_norm_g': 3.27, 'b_group': 17.548, 'b_expert': 11.849, 'ln_f_g': 8.171, 'ln2_g': 3.125}
    for name, (base, spread) in spreads.items():
        noise = np.random.default_rng([zlib.crc32(name.encode()), seed]).standard_normal(out[name].shape)
        drawn = base * np.exp(spread * noise) if base else spread * noise
        out[name] = __import__('jax').numpy.asarray(drawn.astype(out[name].dtype))
    for name, factor in factors.items():
        out[name] = (out[name] * factor).astype(out[name].dtype)
    return out
```

```python
from contextlib import ExitStack

import numpy as np

import concourse.bass as bass
from concourse import mybir

F32 = mybir.dt.float32
F32R = mybir.dt.float32r
I32 = mybir.dt.int32
U32 = mybir.dt.uint32
ALU = mybir.AluOpType
ACT = mybir.ActivationFunctionType
X = mybir.AxisListType.X

P = 128
T = 1024
D = 1024
NT = T // P
KD = D // P
HALF = 512
NH = T // HALF
SB_HEADS, SB_DIM = 8, 64
SB_PAIRS = SB_HEADS // 2
SB_W = SB_HEADS * SB_DIM
GLA_HEADS, DK, DV = 4, 64, 128
GLA_PAIRS = GLA_HEADS // 2
KW, VW = GLA_HEADS * DK, GLA_HEADS * DV
RANK = 16
TAU = 16.0
D_IN = 3 * SB_W + 2 * KW + 2 * VW + RANK
COL_SB_Q, COL_SB_K, COL_SB_V = 0, SB_W, 2 * SB_W
COL_G_Q = 3 * SB_W
COL_G_K = COL_G_Q + KW
COL_G_V = COL_G_K + KW
COL_G_R = COL_G_V + VW
COL_LR = D_IN - P
LEVELS = 7
GROUPS, PER_GROUP = 4, 8
EXPERTS = GROUPS * PER_GROUP
LOGITS = GROUPS + EXPERTS
FF = 512
KF = FF // P
CAP = 96
MAX_BLOCKS = EXPERTS + 2 * T // (CAP + 1)
EPS = 1e-6
SCALE = SB_DIM ** -0.5
FAR = 4096.0


class Chain:

    def __init__(self, eng, sem):
        self.eng, self.sem, self.at, self.n = eng, sem, 0, 0

    def mark(self, ins):
        ins.then_inc(self.sem, 1)
        self.n += 1

    def join(self):
        self.eng.wait_ge(self.sem, self.at + self.n)

    def step(self, ins):
        self.mark(ins)
        self.join()

    def enter(self, i, per):
        base = self.at + self.n
        self.at, self.n = base + i * per, 0
        return base

    def leave(self, base, per, times):
        assert self.n == per, (self.n, per)
        self.at, self.n = base + per * times, 0


def build(nc, a):
    with ExitStack() as ctx:
        _build(nc, ctx, a)


def _build(nc, ctx, a):
    def sb(name, shape, dt=F32, c=ctx):
        return c.enter_context(nc.sbuf_tensor(name, shape, dt))

    def sem(name, c=None):
        return ctx.enter_context(nc.semaphore(name))

    def dram(name, shape):
        return nc.dram_tensor(name, shape, F32)

    ps = ctx.enter_context(nc.psum_tensor("ps", [P, 8, HALF], F32))

    x1_dram = dram("x1_dram", [T, D])
    h2_dram = dram("h2_dram", [T, D])
    y2_dram = dram("y2_dram", [2 * T, D])

    ident = sb("ident", [P, P])
    ones = sb("ones", [P, P])
    eps_t = sb("eps_t", [P, 1])

    chain_v = sem("chain_v")
    chain_g = sem("chain_g")
    chain_a = sem("chain_a")
    made = sem("made")
    V = Chain(nc.vector, chain_v)
    G = Chain(nc.gpsimd, chain_g)
    A = Chain(nc.scalar, chain_a)
    k = dict(nc=nc, sb=sb, sem=sem, ps=ps, a=a, ident=ident, ones=ones, eps_t=eps_t, V=V, G=G, A=A,
             x1_dram=x1_dram, h2_dram=h2_dram, y2_dram=y2_dram)

    with nc.Block() as block:
        @block.gpsimd
        def _(pool):
            G.step(pool.memset(ident[:], 0.0))
            pool.affine_select(out=ident[:], in_=ident[:], compare_op=ALU.not_equal, fill=1.0, base=0,
                               pattern=[[-1, P]], channel_multiplier=1).then_inc(made, 1)
            pool.memset(ones[:], 1.0).then_inc(made, 1)
            pool.memset(eps_t[:], EPS).then_inc(made, 1)
            pool.wait_ge(made, 3)

    logits = sb("logits", [P, NT, LOGITS])
    with ExitStack() as c:
        cat = sb("cat", [P, KD, T], F32, c)
        with ExitStack() as front:
            h_hi = sb("h_hi", [P, KD, T], F32R, front)
            h_lo = sb("h_lo", [P, KD, T], F32R, front)
            with ExitStack() as c2:
                norm_and_turn(k, c2, h_hi, h_lo)
            with ExitStack() as c2:
                stick_breaking(k, c2, h_hi, h_lo, cat)
            with ExitStack() as c2:
                linear_attention(k, c2, h_hi, h_lo, cat)
        mix_out(k, c, cat, logits)
    with ExitStack() as c:
        tables = route(k, c, logits)
        experts(k, c, tables)
    with ExitStack() as c:
        combine(k, c)


def bank(k, i, n=HALF, p=P):
    return k["ps"][0:p, i, 0:n]


def norm_and_turn(k, c, h_hi, h_lo):
    nc, sb, sem, ps, a, ident, V, A = (k[n] for n in ("nc", "sb", "sem", "ps", "a", "ident", "V", "A"))
    xt = sb("xt", [P, NT, D], F32, c)
    xn = sb("xn", [P, NT, D], F32, c)
    squares = sb("squares", [P, D], F32, c)
    ss = sb("ss", [P, NT], F32, c)
    rms = sb("rms", [P, NT], F32, c)
    inv = sb("inv", [P, NT], F32, c)
    g1 = sb("g1", [P, KD], F32, c)
    x_in = [sem(f"x_in{t}", c) for t in range(NT)]
    g_in = sem("g_in", c)
    rms_done, inv_done, xn_done = sem("rms_done", c), sem("inv_done", c), sem("xn_done", c)
    turned, hi_done, lo_done = sem("turned", c), sem("hi_done", c), sem("lo_done", c)
    groups = [(hf, kd) for hf in range(NH) for kd in range(KD)]
    per = NT // NH
    with nc.Block() as block:
        @block.sync
        def _(sp):
            for t in range(NT):
                sp.dma_start(xt[:, t, :], a["x"][0, t * P:(t + 1) * P, :]).then_inc(x_in[t], 16)
            with nc.allow_non_contiguous_dma(reason="a thousand gains, features to partitions"):
                sp.dma_start(g1[:], a["ln1_g"][0].rearrange("(k p) -> p k", p=P)).then_inc(g_in, 16)

        @block.scalar
        def _(act):
            for t in range(NT):
                act.wait_ge(x_in[t], 16)
                A.step(act.activation(squares[:], xt[:, t, :], ACT.Square, accum_out=ss[:, t:t + 1]))
            act.activation(rms[:], ss[:], ACT.Sqrt, bias=k["eps_t"][:], scale=1.0 / D).then_inc(rms_done, 1)
            act.wait_ge(g_in, 16)
            for n, (hf, kd) in enumerate(groups):
                act.wait_ge(turned, n + 1)
                act.activation(h_hi[:, kd, hf * HALF:(hf + 1) * HALF], bank(k, n % 4), ACT.Copy,
                               scale=g1[:, kd:kd + 1]).then_inc(hi_done, 1)

        @block.vector
        def _(dve):
            dve.wait_ge(rms_done, 1)
            V.step(dve.reciprocal(inv[:], rms[:]))
            for t in range(NT):
                dve.tensor_scalar(xn[:, t, :], xt[:, t, :], inv[:, t:t + 1], None, ALU.mult).then_inc(xn_done, 1)
            dve.wait_ge(g_in, 16)
            for n, (hf, kd) in enumerate(groups):
                dve.wait_ge(hi_done, n + 1)
                cols = slice(hf * HALF, (hf + 1) * HALF)
                dve.scalar_tensor_tensor(h_lo[:, kd, cols], bank(k, n % 4), g1[:, kd:kd + 1],
                                         h_hi[:, kd, cols].bitcast(F32), ALU.mult,
                                         ALU.subtract).then_inc(lo_done, 1)

        @block.tensor
        def _(pe):
            for n, (hf, kd) in enumerate(groups):
                if kd == 0:
                    pe.wait_ge(xn_done, per * (hf + 1))
                if n >= 4:
                    pe.wait_ge(lo_done, n - 3)
                for j in range(per):
                    mm = pe.transpose(k["ps"][:, n % 4, j * P:(j + 1) * P],
                                      xn[:, hf * per + j, kd * P:(kd + 1) * P], ident[:])
                mm.then_inc(turned, 1)


def project(pe, k, w_hi, w_lo, h_hi, h_lo, half, out):
    cols = slice(half * HALF, (half + 1) * HALF)
    n = 0
    for kd in range(KD):
        for w, h in ((w_hi, h_hi), (w_hi, h_lo), (w_lo, h_hi)):
            mm = pe.matmul(out, w[:, kd, :], h[:, kd, cols], start=(n == 0), stop=(n == 3 * KD - 1))
            n += 1
    return mm


def stick_breaking(k, c, h_hi, h_lo, cat):
    nc, sb, sem, ps, a, ident, V, A, G = (k[n] for n in ("nc", "sb", "sem", "ps", "a", "ident", "V", "A", "G"))
    w_raw = sb("w_raw", [P, 3, KD, P], F32, c)
    w_hi = sb("w_hi", [P, 3, KD, P], F32R, c)
    w_lo = sb("w_lo", [P, 3, KD, P], F32R, c)
    qkv = sb("qkv", [P, 3, T], F32, c)
    v = sb("v", [P, NT, P], F32, c)
    stay = sb("stay", [P, 2, T], F32, c)
    beta = sb("beta", [P, 2, T], F32, c)
    prod = sb("prod", [P, 2, T + 1], F32, c)
    wt = sb("wt", [P, 2, T], F32, c)
    wT = sb("wT", [P, 2, T], F32, c)
    o = sb("o", [P, NT, P], F32, c)
    w_in_s = [sem(f"sbw_in{j}", c) for j in range(3)]
    names = "sb_hi sb_lo sb_proj sb_qkv sb_vturn sb_v sb_z sb_sig sb_masked " \
            "sb_scan sb_w sb_wturn sb_wT sb_pv sb_o sb_oturn sb_cat sb_one sb_passed".split()
    (hi_done, lo_done, projd, qkv_done, vturn, v_done, z_done, sig_done, masked,
     scan_done, w_done, wturn, wT_done, pv_done, o_done, oturn, cat_done, one, passed) = (sem(n, c) for n in names)
    U = 2 * NT
    units = [(i, h) for i in range(NT) for h in range(2)]
    nturn = [(i + 4) // 4 for i, h in units]
    before = [sum(nturn[:u]) for u in range(U)]
    TURNS = sum(nturn)
    w_dram = a["w_in"][0].rearrange("(k p) c -> p k c", p=P)
    col0 = (COL_SB_Q, COL_SB_K, COL_SB_V)

    def nk(i):
        return (i + 1) * P

    with nc.Block() as block:
        @block.sync
        def _(sp):
            with sp.Fori(0, SB_PAIRS) as p:
                for j in range(3):
                    sp.wait_ge(lo_done, 3 * p + j + 1)
                    sp.dma_start(w_raw[:, j], w_dram[:, :, bass.ds(p * P + col0[j], P)]).then_inc(w_in_s[j], 16)

        @block.scalar
        def _(act):
            with act.Fori(0, SB_PAIRS) as p:
                for j in range(3):
                    act.wait_ge(w_in_s[j], 16 * p + 16)
                    act.wait_ge(projd, 6 * p + 2 * j + 2)
                    act.activation(w_hi[:, j], w_raw[:, j], ACT.Copy).then_inc(hi_done, 1)
                for n in range(6):
                    act.wait_ge(projd, 6 * p + n + 7)
                    j, hf = divmod(n, 2)
                    act.activation(qkv[:, j, hf * HALF:(hf + 1) * HALF], bank(k, n % 4), ACT.Copy).then_inc(qkv_done, 1)
                for u, (i, h) in enumerate(units):
                    act.wait_ge(z_done, U * p + u + 1)
                    act.wait_ge(w_done, U * p + u + 1)
                    z = ps[:, 2 * (u % 2):2 * (u % 2) + 2, :].rearrange("p b n -> p (b n)")[:, 0:nk(i)]
                    act.activation(stay[:, u % 2, 0:nk(i)], z, ACT.Sigmoid, scale=-SCALE).then_inc(sig_done, 1)
                    act.activation(beta[:, u % 2, 0:nk(i)], z, ACT.Sigmoid, scale=SCALE).then_inc(sig_done, 1)

        @block.gpsimd
        def _(pool):
            pool.memset(prod[:, :, T:T + 1], 1.0).then_inc(one, 1)
            fill_one, fill_zero = pool.to_reg(1.0), pool.to_reg(0.0)
            pool.sem_inc(w_done, 2)
            with pool.Fori(0, SB_PAIRS) as p:
                for u, (i, h) in enumerate(units):
                    b = u % 2
                    diag = slice(i * P, (i + 1) * P)
                    pool.wait_ge(sig_done, 2 * U * p + 2 * u + 1)
                    pool.sem_inc(passed, 1)
                    pool.affine_select(out=stay[:, b, diag], in_=stay[:, b, diag], compare_op=ALU.is_gt,
                                       fill=fill_one, base=0, pattern=[[-1, P]], channel_multiplier=1).then_inc(masked, 1)
                    pool.wait_ge(sig_done, 2 * U * p + 2 * u + 2)
                    pool.sem_inc(passed, 1)
                    pool.affine_select(out=beta[:, b, diag], in_=beta[:, b, diag], compare_op=ALU.is_gt,
                                       fill=fill_zero, base=0, pattern=[[-1, P]], channel_multiplier=1).then_inc(masked, 1)
                    pool.wait_ge(masked, 2 * U * p + 2 * u + 2)
                    pool.wait_ge(scan_done, U * p + u + 1)
                    pool.wait_ge(wturn, TURNS * p + 4 + (before[u - 1] if u else -nturn[U - 1]))
                    pool.tensor_tensor(wt[:, b, 0:nk(i)], beta[:, b, 0:nk(i)], prod[:, b, T + 1 - nk(i):T + 1],
                                       ALU.mult).then_inc(w_done, 1)

        @block.vector
        def _(dve):
            dve.sem_inc(lo_done, 3)
            dve.sem_inc(cat_done, 2)
            dve.wait_ge(one, 1)
            with dve.Fori(0, SB_PAIRS) as p:
                for j in range(3):
                    dve.wait_ge(hi_done, 3 * p + j + 1)
                    dve.tensor_tensor(w_lo[:, j], w_raw[:, j], w_hi[:, j].bitcast(F32), ALU.subtract)\
                       .then_inc(lo_done, 1)
                for n in range(2):
                    dve.wait_ge(vturn, 2 * p + n + 1)
                    dve.tensor_copy(v[:, 4 * n:4 * n + 4, :].rearrange("p t n -> p (t n)"), bank(k, 4 + n)).then_inc(v_done, 1)
                for u in range(U + 1):
                    if u < U:
                        i, h = units[u]
                        dve.wait_ge(masked, 2 * U * p + 2 * u + 1)
                        dve.wait_ge(w_done, U * p + u + 1)
                        dve.tensor_tensor_scan(prod[:, u % 2, T - nk(i):T][:, ::-1], stay[:, u % 2, 0:nk(i)][:, ::-1],
                                               stay[:, u % 2, 0:nk(i)][:, ::-1], 1.0, ALU.mult,
                                               ALU.bypass).then_inc(scan_done, 1)
                    if u >= 1:
                        i, h = units[u - 1]
                        for m in range(nturn[u - 1]):
                            w0, w1 = 4 * P * m, min(4 * P * (m + 1), nk(i))
                            n = before[u - 1] + m
                            dve.wait_ge(wturn, TURNS * p + n + 1 + 4)
                            dve.wait_ge(pv_done, U * p + u)
                            dve.tensor_copy(wT[:, (u - 1) % 2, w0:w1], bank(k, 4 + n % 2, w1 - w0)).then_inc(wT_done, 1)
                for n in range(2):
                    dve.wait_ge(pv_done, U * p + U + 2)
                    dve.tensor_copy(o[:, 4 * n:4 * n + 4, :].rearrange("p t n -> p (t n)"), bank(k, 6 + n)).then_inc(o_done, 1)
                for n in range(2):
                    dve.wait_ge(oturn, 2 * p + n + 1)
                    dve.tensor_copy(cat[:, bass.ds(p, 1), n * HALF:(n + 1) * HALF].rearrange("p o n -> p (o n)"),
                                    bank(k, 4 + n)).then_inc(cat_done, 1)

        @block.tensor
        def _(pe):
            pe.sem_inc(projd, 6)
            pe.sem_inc(pv_done, 2)
            pe.sem_inc(wturn, 4)
            with pe.Fori(0, SB_PAIRS) as p:
                for n in range(6):
                    j, hf = divmod(n, 2)
                    if hf == 0:
                        pe.wait_ge(lo_done, 3 * p + j + 4)
                    if n >= 4:
                        pe.wait_ge(qkv_done, 6 * p + n - 3)
                    project(pe, k, w_hi[:, j], w_lo[:, j], h_hi, h_lo, hf, bank(k, n % 4)).then_inc(projd, 1)
                pe.wait_ge(cat_done, 2 * p + 2)
                for n in range(2):
                    pe.wait_ge(qkv_done, 6 * p + 5 + n)
                    for m in range(4):
                        mm = pe.transpose(ps[:, 4 + n, m * P:(m + 1) * P],
                                          qkv[:, 2, (4 * n + m) * P:(4 * n + m + 1) * P], ident[:])
                    mm.then_inc(vturn, 1)
                for u in range(U + 3):
                    if u < U:
                        i, h = units[u]
                        if u >= 2:
                            pe.wait_ge(sig_done, 2 * U * p + 2 * (u - 1))
                        rows = slice(SB_DIM * h, SB_DIM * (h + 1))
                        for s in range(0, nk(i), HALF):
                            e = min(s + HALF, nk(i))
                            mm = pe.matmul(bank(k, 2 * (u % 2) + s // HALF, e - s), qkv[rows, 0, i * P:(i + 1) * P],
                                           qkv[rows, 1, s:e], start=True, stop=True)
                        mm.then_inc(z_done, 1)
                    if 2 <= u < U + 2:
                        i, h = units[u - 2]
                        pe.wait_ge(w_done, U * p + u - 1 + 2)
                        for m in range(nturn[u - 2]):
                            n = before[u - 2] + m
                            if n >= 2:
                                pe.wait_ge(wT_done, TURNS * p + n - 1)
                            else:
                                pe.wait_ge(v_done, 2 * p + n + 1)
                            for q in range(4 * m, min(4 * m + 4, i + 1)):
                                mm = pe.transpose(ps[:, 4 + n % 2, (q - 4 * m) * P:(q - 4 * m + 1) * P],
                                                  wt[:, (u - 2) % 2, q * P:(q + 1) * P], ident[:])
                            mm.then_inc(wturn, 1)
                    if u >= 3:
                        i, h = units[u - 3]
                        pe.wait_ge(wT_done, TURNS * p + before[u - 3] + nturn[u - 3])
                        if u == 3:
                            pe.wait_ge(v_done, 2 * p + 2)
                        for q in range(i + 1):
                            mm = pe.matmul(ps[:, 6 + i // 4, (i % 4) * P + SB_DIM * h:(i % 4) * P + SB_DIM * (h + 1)],
                                           wT[:, (u - 3) % 2, q * P:(q + 1) * P], v[:, q, SB_DIM * h:SB_DIM * (h + 1)],
                                           start=(q == 0), stop=(q == i))
                        mm.then_inc(pv_done, 1)
                for n in range(2):
                    pe.wait_ge(o_done, 2 * p + n + 1)
                    for m in range(4):
                        mm = pe.transpose(ps[:, 4 + n, m * P:(m + 1) * P], o[:, 4 * n + m, :], ident[:])
                    mm.then_inc(oturn, 1)


def linear_attention(k, c, h_hi, h_lo, cat):
    nc, sb, sem, ps, a, ident, ones, V, A, G = (
        k[n] for n in ("nc", "sb", "sem", "ps", "a", "ident", "ones", "V", "A", "G"))
    w_raw = sb("gw_raw", [P, 2, KD, P], F32, c)
    w_hi = sb("gw_hi", [P, 2, KD, P], F32R, c)
    w_lo = sb("gw_lo", [P, 2, KD, P], F32R, c)
    b_all = sb("b_all", [P, 2, T], F32, c)
    b = sb("b", [P, T], F32, c)
    qk = sb("qk", [P, 2, T], F32, c)
    vT = sb("vT", [P, 2, T], F32, c)
    v = sb("gv", [P, NT, 2 * DV], F32, c)
    r = sb("r", [P, 2, T], F32, c)
    e = sb("e", [P, 2, T], F32, c)
    ql = sb("ql", [P, 2, T // 2], F32, c)
    kl = sb("kl", [P, 2, T], F32, c)
    s_all = sb("s_all", [P, 2, NT, P], F32, c)
    k_dec = sb("k_dec", [P, NT, P], F32, c)
    e_last = sb("e_last", [P, NT], F32, c)
    state = sb("state", [P, 2, DV], F32, c)
    masks = sb("masks", [P, LEVELS, P // 2], F32, c)
    w2 = sb("w2", [P, KW], F32, c)
    gb = sb("gb", [P, GLA_PAIRS], F32, c)
    gn = sb("gn", [P, GLA_HEADS], F32, c)
    gn_p = sb("gn_p", [P, 2], F32, c)
    w_in_s = [sem(f"gw_in{j}") for j in range(2)]
    small = sem("g_small")
    names = "g_made g_hi g_lo g_proj g_out g_rdone g_vturn g_v g_decay g_dec_e g_dec g_kturn g_kdec g_dif g_exp " \
            "g_ql g_lev g_pred g_upd g_state g_o g_sq g_sum g_rms g_cat g_lr g_u g_x g_ln g_passed".split()
    (made, hi_done, lo_done, projd, out_done, r_done, vturn, v_done, decay, dec_e, dec, kturn, kdec_done, dif,
     exp_done, ql_done, lev_done, pred_done, upd, state_done, o_ready, sq_done, summed, rms_done, cat_done,
     lr_done, u_done, x_done, ln_done, passed) = (sem(n) for n in names)
    w_dram = a["w_in"][0].rearrange("(k p) c -> p k c", p=P)
    TILES = 6
    PREDS = 4 + 2 * LEVELS
    cols = [(COL_G_Q, P), (COL_G_K, P), (COL_G_V, 2 * P), (COL_G_V + P, 2 * P), (COL_G_R, 2 * P), (COL_G_R + P, 2 * P)]

    def halves(ap, l):
        n = 1 << l
        return ap.rearrange("p (b two n) -> p b two n", two=2, n=n)

    with nc.Block() as block:
        @block.sync
        def _(sp):
            sp.dma_start(w_raw[:, 1], w_dram[:, :, COL_LR:COL_LR + P]).then_inc(w_in_s[1], 16)
            sp.wait_ge(made, 1)
            sp.dma_start(w2[P - RANK:P, :], a["gla_gate_w2"][0]).then_inc(small, 16)
            with nc.allow_non_contiguous_dma(reason="biases and gains to partitions"):
                sp.dma_start(gb[:], a["gla_gate_b"][0].rearrange("(k p) -> p k", p=P)).then_inc(small, 16)
                sp.dma_start(gn[:], a["gla_norm_g"][0].rearrange("(k p) -> p k", p=P)).then_inc(small, 16)
            with sp.Fori(0, GLA_PAIRS) as p:
                for j, (c0, step) in enumerate(cols):
                    sp.wait_ge(lo_done, TILES * p + j + 1)
                    sp.dma_start(w_raw[:, j % 2], w_dram[:, :, bass.ds(p * step + c0, P)]).then_inc(w_in_s[j % 2], 16)

        @block.gpsimd
        def _(pool):
            pool.memset(w2[:], 0.0).then_inc(made, 1)
            pool.memset(kl[:], 0.0).then_inc(made, 1)
            G.step(pool.memset(masks[:], 1.0))
            for l in range(LEVELS):
                n = 1 << l
                nb = P // (2 * n)
                m = masks[:, l, :].rearrange("p (b n) -> p b n", n=n)
                lo, hi = [[-2 * n, nb]], [[2 * n, nb]]
                if nb == 1:
                    m, lo, hi = masks[:, l, :], [], []
                if n > 1:
                    lo, hi = lo + [[0, n]], hi + [[0, n]]
                else:
                    m = masks[:, l, :]
                G.step(pool.affine_select(out=m, in_=m, compare_op=ALU.is_ge, fill=0.0, base=0,
                                          pattern=lo, channel_multiplier=1))
                G.step(pool.affine_select(out=m, in_=m, compare_op=ALU.is_ge, fill=0.0, base=n - 1,
                                          pattern=hi, channel_multiplier=-1))
            pool.memset(s_all[:], 0.0).then_inc(made, 1)
            with pool.Fori(0, GLA_PAIRS) as p:
                pool.wait_ge(dec_e, 3 * p + 3)
                pool.wait_ge(v_done, 4 * p + 4)
                pool.tensor_tensor(vT[:, 0], qk[:, 0], e[:, 0], ALU.mult).then_inc(dec, 1)
                pool.tensor_tensor(vT[:, 1], qk[:, 1], e[:, 1], ALU.mult).then_inc(dec, 1)
                for l in range(LEVELS):
                    pool.wait_ge(exp_done, LEVELS * p + l + 1)
                    if l >= 2:
                        pool.wait_ge(lev_done, (LEVELS + 1) * p + l)
                    n = 1 << l
                    pool.tensor_tensor(ql[:, l % 2].rearrange("p (b n) -> p b n", n=n),
                                       halves(qk[:, 0], l)[:, :, 1, :], halves(e[:, l % 2], l)[:, :, 1, :],
                                       ALU.mult).then_inc(ql_done, 1)
                    pool.tensor_tensor(halves(kl[:, l % 2], l)[:, :, 0, :], halves(qk[:, 1], l)[:, :, 0, :],
                                       halves(e[:, l % 2], l)[:, :, 0, :], ALU.mult).then_inc(ql_done, 1)

        def evict_projection(act, p, j):
            for hf in range(2):
                n = 2 * j + hf
                act.wait_ge(projd, 2 * TILES * p + n + 1 + 2)
                dst = slice(hf * HALF, (hf + 1) * HALF)
                if j < 2:
                    act.activation(qk[:, j, dst], bank(k, n % 4), ACT.Copy,
                                   scale=DK ** -0.5 if j == 0 else 1.0).then_inc(out_done, 1)
                elif j < 4:
                    act.activation(vT[:, j - 2, dst], bank(k, n % 4), ACT.Copy).then_inc(out_done, 1)
                else:
                    act.activation(r[:, j - 4, dst], bank(k, n % 4), ACT.Sigmoid).then_inc(out_done, 1)

        @block.scalar
        def _(act):
            act.wait_ge(w_in_s[1], 16)
            act.activation(w_hi[:, 1], w_raw[:, 1], ACT.Copy).then_inc(hi_done, 1)
            for n in range(2):
                act.wait_ge(projd, n + 1)
                act.activation(vT[:, 0, n * HALF:(n + 1) * HALF], bank(k, n), ACT.Copy).then_inc(lr_done, 1)
            act.wait_ge(x_done, 4)
            A.step(act.activation(e[:], b_all[:], ACT.Abs))
            A.step(act.activation(e[:], e[:], ACT.Exp, scale=-1.0))
            act.activation(e[:], e[:], ACT.Ln, bias=1.0).then_inc(ln_done, 1)
            with act.Fori(0, GLA_PAIRS) as p:
                for j in range(TILES):
                    act.wait_ge(w_in_s[j % 2], 16 * (TILES // 2) * p + 16 * (j // 2 + 1) + 16 * (j % 2))
                    act.wait_ge(projd, 2 * TILES * p + 2 * j + 1)
                    act.activation(w_hi[:, j % 2], w_raw[:, j % 2], ACT.Copy).then_inc(hi_done, 1)
                    if j >= 1:
                        evict_projection(act, p, j - 1)
                evict_projection(act, p, TILES - 1)
                act.wait_ge(decay, p + 1)
                act.activation(e[:, 0], b[:], ACT.Exp).then_inc(dec_e, 1)
                act.activation(e_last[:], b[:, P - 1:T:P], ACT.Exp).then_inc(dec_e, 1)
                act.activation(e[:, 1], e[:, 1], ACT.Exp).then_inc(dec_e, 1)
                for l in range(LEVELS):
                    act.wait_ge(dif, 2 * LEVELS * p + 2 * l + 2)
                    act.activation(e[:, l % 2], e[:, l % 2], ACT.Exp).then_inc(exp_done, 1)
                act.wait_ge(o_ready, NT * p + NT)
                for h in range(2):
                    o = ps[:, 2 * h:2 * h + 2, :].rearrange("p b n -> p (b n)")
                    act.activation(e[:, h], o, ACT.Square).then_inc(sq_done, 1)
                for h in range(2):
                    act.wait_ge(summed, 2 * p + h + 1)
                    s = ps[:, 4 + 2 * h:6 + 2 * h, :].rearrange("p b n -> p (b n)")
                    act.activation(kl[:, h], s, ACT.Sqrt, bias=k["eps_t"][:], scale=1.0 / DV).then_inc(rms_done, 1)

        @block.vector
        def _(dve):
            dve.sem_inc(lo_done, 1)
            dve.wait_ge(made, 3)
            dve.wait_ge(hi_done, 1)
            dve.tensor_tensor(w_lo[:, 1], w_raw[:, 1], w_hi[:, 1].bitcast(F32), ALU.subtract).then_inc(lo_done, 1)
            for n in range(4):
                pr, hf = divmod(n, 2)
                dve.wait_ge(u_done, n + 1)
                dve.wait_ge(small, 48)
                dve.tensor_scalar(b_all[:, pr, hf * HALF:(hf + 1) * HALF], bank(k, 4 + n), gb[:, pr:pr + 1], None,
                                  ALU.add).then_inc(x_done, 1)
            dve.wait_ge(x_done, 4)
            dve.wait_ge(ln_done, 1)
            V.step(dve.tensor_scalar(b_all[:], b_all[:], 0.0, None, ALU.min))
            V.step(dve.tensor_tensor(b_all[:], b_all[:], e[:], ALU.subtract))
            V.step(dve.tensor_scalar(b_all[:], b_all[:], 1.0 / TAU, None, ALU.mult))
            for pr in range(2):
                for t in range(NT):
                    x = b_all[:, pr, t * P:(t + 1) * P]
                    V.mark(dve.tensor_tensor_scan(e[:, pr, t * P:(t + 1) * P], x, x, 0.0, ALU.add, ALU.bypass))
            V.join()
            V.step(dve.tensor_copy(b_all[:], e[:]))
            PER = 6
            dve.sem_inc(cat_done, 2)
            with dve.Fori(0, GLA_PAIRS) as p:
                base = V.enter(p, PER)
                dve.wait_ge(cat_done, 2 * p + 2)
                for j in range(TILES):
                    dve.wait_ge(hi_done, TILES * p + j + 2)
                    dve.tensor_tensor(w_lo[:, j % 2], w_raw[:, j % 2], w_hi[:, j % 2].bitcast(F32), ALU.subtract)\
                       .then_inc(lo_done, 1)
                    if j == 0:
                        V.mark(dve.tensor_copy(gn_p[:], gn[:, bass.ds(2 * p, 2)]))
                        V.step(dve.tensor_copy(b[:], b_all[:, bass.ds(p, 1), :].rearrange("p o n -> p (o n)")))
                for j in range(2):
                    for hf in range(2):
                        dst = slice(hf * HALF, (hf + 1) * HALF)
                        n = 8 + 2 * j + hf
                        dve.wait_ge(out_done, 2 * TILES * p + n + 1)
                        dve.tensor_tensor(r[:, j, dst], bank(k, n % 4), r[:, j, dst], ALU.mult).then_inc(r_done, 1)
                bt = b[:].rearrange("p (t n) -> p t n", n=P)
                dve.tensor_tensor(e[:, 1].rearrange("p (t n) -> p t n", n=P), bt[:, :, P - 1:P].to_broadcast([P, NT, P]),
                                  bt, ALU.subtract).then_inc(decay, 1)
                for n in range(4):
                    dve.wait_ge(vturn, 4 * p + n + 1)
                    dve.tensor_copy(v[:, 2 * n:2 * n + 2, :].rearrange("p t n -> p (t n)"), bank(k, 4 + n)).then_inc(v_done, 1)
                for n in range(2):
                    dve.wait_ge(kturn, 2 * p + n + 1)
                    dve.tensor_copy(k_dec[:, 4 * n:4 * n + 4, :].rearrange("p t n -> p (t n)"), bank(k, 4 + n))\
                       .then_inc(kdec_done, 1)
                dve.wait_ge(lev_done, (LEVELS + 1) * p + 1)
                dve.sem_inc(passed, 1)
                eye = ident[:].bitcast(I32).unsqueeze(1).to_broadcast([P, 4, P])
                for m in range(4):
                    dst = s_all[:, m // 2, 4 * (m % 2):4 * (m % 2) + 4, :]
                    dve.copy_predicated(dst, eye, bank(k, m).rearrange("p (q n) -> p q n", n=P)).then_inc(pred_done, 1)
                for l in range(LEVELS + 1):
                    if l < LEVELS:
                        if l < 2:
                            dve.wait_ge(dec, 2 * p + 2)
                        else:
                            dve.wait_ge(ql_done, 2 * LEVELS * p + 2 * (l - 2) + 2)
                        bl = halves(b[:], l)
                        el = halves(e[:, l % 2], l)
                        n, nb = 1 << l, T >> (l + 1)
                        ref = bl[:, :, 0, n - 1:n].to_broadcast([P, nb, n])
                        dve.tensor_tensor(el[:, :, 0, :], ref, bl[:, :, 0, :], ALU.subtract).then_inc(dif, 1)
                        dve.tensor_tensor(el[:, :, 1, :], bl[:, :, 1, :], ref, ALU.subtract).then_inc(dif, 1)
                    if l >= 1:
                        m = l - 1
                        n, nb = 1 << m, P >> (m + 1)
                        dve.wait_ge(lev_done, (LEVELS + 1) * p + m + 2)
                        for h in range(2):
                            dst = halves(s_all[:, h].rearrange("p t n -> p (t n)"), m)[:, :, 1, :]
                            dst = dst.rearrange("p (q b) n -> p q b n", q=NT)
                            msk = masks[:, m, :].bitcast(I32).rearrange("p (b n) -> p b n", n=n).unsqueeze(1)\
                                .to_broadcast([P, NT, nb, n])
                            src = bank(k, 4 + 2 * (m % 2) + h).rearrange("p (q b n) -> p q b n", q=8, n=n)
                            dve.wait_ge(pred_done, PREDS * p + 4 + 2 * m)
                            dve.sem_inc(passed, 1)
                            dve.copy_predicated(dst, msk, src).then_inc(pred_done, 1)
                for t in range(NT):
                    dve.wait_ge(upd, NT * p + t + 1)
                    for h in range(2):
                        rows = slice(DK * h, DK * (h + 1))
                        new = bank(k, 4 + t % 2)[rows, h * DV:(h + 1) * DV]
                        if t == 0:
                            ins = dve.tensor_copy(state[rows, 1, :], new)
                        else:
                            if h == 0:
                                dve.wait_ge(state_done, 2 * NT * p + 2 * t)
                                if t >= 2:
                                    dve.wait_ge(o_ready, NT * p + t)
                            ins = dve.scalar_tensor_tensor(state[rows, (t + 1) % 2, :], state[rows, t % 2, :],
                                                           e_last[rows, t:t + 1], new, ALU.mult, ALU.add)
                        ins.then_inc(state_done, 1)
                for h in range(2):
                    dve.wait_ge(rms_done, 2 * p + h + 1)
                    V.step(dve.reciprocal(kl[:, h], kl[:, h]))
                    o = ps[:, 2 * h:2 * h + 2, :].rearrange("p b n -> p (b n)")
                    V.step(dve.tensor_tensor(e[:, h], o, kl[:, h], ALU.mult))
                    dve.scalar_tensor_tensor(cat[:, bass.ds(2 * p + (SB_PAIRS + h), 1), :].rearrange("p o n -> p (o n)"),
                                             e[:, h], gn_p[:, h:h + 1], r[:, h], ALU.mult, ALU.mult).then_inc(cat_done, 1)
                V.leave(base, PER, GLA_PAIRS)

        @block.tensor
        def _(pe):
            for hf in range(2):
                pe.wait_ge(lo_done, 2)
                project(pe, k, w_hi[:, 1], w_lo[:, 1], h_hi, h_lo, hf, bank(k, hf)).then_inc(projd, 1)
            pe.wait_ge(small, 48)
            pe.wait_ge(lr_done, 2)
            for n in range(4):
                pr, hf = divmod(n, 2)
                pe.matmul(bank(k, 4 + n), w2[:, pr * P:(pr + 1) * P], vT[:, 0, hf * HALF:(hf + 1) * HALF],
                          start=True, stop=True).then_inc(u_done, 1)
            pe.wait_ge(x_done, 4)
            with pe.Fori(0, GLA_PAIRS) as p:
                pe.wait_ge(cat_done, 2 * p + 2)
                for n in range(2 * TILES):
                    j, hf = divmod(n, 2)
                    if hf == 0:
                        pe.wait_ge(lo_done, TILES * p + j + 3)
                    if n >= 4:
                        pe.wait_ge(out_done, 2 * TILES * p + n - 3)
                    project(pe, k, w_hi[:, j % 2], w_lo[:, j % 2], h_hi, h_lo, hf, bank(k, n % 4)).then_inc(projd, 1)
                pe.wait_ge(out_done, 2 * TILES * p + 8)
                for n in range(4):
                    for m in range(4):
                        t, h = 2 * n + m // 2, m % 2
                        mm = pe.transpose(ps[:, 4 + n, m * P:(m + 1) * P], vT[:, h, t * P:(t + 1) * P], ident[:])
                    mm.then_inc(vturn, 1)
                pe.wait_ge(r_done, 4 * p + 4)
                for t in range(NT):
                    for h in range(2):
                        rows = slice(DK * h, DK * (h + 1))
                        mm = pe.matmul(ps[:, 2 * h + t // 4, (t % 4) * P:(t % 4 + 1) * P], qk[rows, 1, t * P:(t + 1) * P],
                                       qk[rows, 0, t * P:(t + 1) * P], start=True, stop=True)
                mm.then_inc(lev_done, 1)
                pe.wait_ge(dec, 2 * p + 2)
                for n in range(2):
                    pe.wait_ge(v_done, 4 * p + n + 1)
                    for m in range(4):
                        mm = pe.transpose(ps[:, 4 + n, m * P:(m + 1) * P], vT[:, 1, (4 * n + m) * P:(4 * n + m + 1) * P],
                                          ident[:])
                    mm.then_inc(kturn, 1)
                pe.wait_ge(kdec_done, 2 * p + 2)
                pe.wait_ge(v_done, 4 * p + 4)
                for l in range(LEVELS):
                    pe.wait_ge(ql_done, 2 * LEVELS * p + 2 * l + 2)
                    if l >= 2:
                        pe.wait_ge(pred_done, PREDS * p + 2 * l + 2)
                    for t in range(NT):
                        for h in range(2):
                            rows = slice(DK * h, DK * (h + 1))
                            mm = pe.matmul(ps[:, 4 + 2 * (l % 2) + h, t * 64:(t + 1) * 64],
                                           kl[rows, l % 2, t * P:(t + 1) * P], ql[rows, l % 2, t * 64:(t + 1) * 64],
                                           start=True, stop=True)
                    mm.then_inc(lev_done, 1)
                pe.wait_ge(pred_done, PREDS * p + PREDS)
                for t in range(NT):
                    if t >= 2:
                        pe.wait_ge(state_done, 2 * NT * p + 2 * (t - 1))
                    if t < NT:
                        pe.matmul(bank(k, 4 + t % 2, 2 * DV), k_dec[:, t, :], v[:, t, :], start=True, stop=True).then_inc(upd, 1)
                    if t >= 1:
                        pe.wait_ge(state_done, 2 * NT * p + 2 * t)
                    for h in range(2):
                        rows = slice(DK * h, DK * (h + 1))
                        out = ps[:, 2 * h + t // 4, (t % 4) * P:(t % 4 + 1) * P]
                        mm = pe.matmul(out, v[:, t, h * DV:(h + 1) * DV], s_all[:, h, t, :], start=True, stop=(t == 0))
                        if t >= 1:
                            mm = pe.matmul(out, state[rows, t % 2, :], vT[rows, 0, t * P:(t + 1) * P],
                                           start=False, stop=True)
                    mm.then_inc(o_ready, 1)
                pe.wait_ge(state_done, 2 * NT * p + 2 * NT)
                for h in range(2):
                    pe.wait_ge(sq_done, 2 * p + h + 1)
                    for hf in range(2):
                        mm = pe.matmul(bank(k, 4 + 2 * h + hf), ones[:], e[:, h, hf * HALF:(hf + 1) * HALF],
                                       start=True, stop=True)
                    mm.then_inc(summed, 1)


def mix_out(k, c, cat, logits):
    nc, sb, sem, ps, a, ident, V, A, G = (k[n] for n in ("nc", "sb", "sem", "ps", "a", "ident", "V", "A", "G"))
    wo_raw = sb("wo_raw", [P, 2, D], F32, c)
    wo_hi = sb("wo_hi", [P, KD, D], F32R, c)
    wo_lo = sb("wo_lo", [P, KD, D], F32R, c)
    cat_hi = sb("cat_hi", [P, 2, KD, P], F32R, c)
    cat_lo = sb("cat_lo", [P, 2, KD, P], F32R, c)
    x = sb("x_res", [P, 2, D], F32, c)
    x1 = sb("x1", [P, 2, D], F32, c)
    sq = sb("sq", [P, D], F32, c)
    h2 = sb("h2", [P, 2, D], F32, c)
    g2 = sb("g2", [P, D], F32, c)
    h2T = sb("h2T", [P, KD, P], F32, c)
    wr = sb("wr", [P, KD, LOGITS], F32, c)
    rb = sb("rb", [P, LOGITS], F32, c)
    ss, rms, inv = (sb(n, [P, 2], F32, c) for n in ("o_ss", "o_rms", "o_inv"))
    wo_in = [sem(f"wo_in{j}") for j in range(2)]
    x_in = [sem(f"xr_in{j}") for j in range(2)]
    x1_out = [sem(f"x1_out{j}") for j in range(2)]
    h2_out = [sem(f"h2_out{j}") for j in range(2)]
    small = sem("o_small")
    names = "o_wohi o_wolo o_cathi o_catlo o_mm o_x1 o_ss o_rms o_inv o_h2 o_turn o_h2T o_lg o_logits".split()
    (wohi, wolo, cathi, catlo, mm_done, x1_done, ss_done, rms_done, inv_done, h2_done, turned, h2T_done, lg,
     logit_done) = (sem(n) for n in names)
    with nc.Block() as block:
        @block.sync
        def _(sp):
            sp.dma_start(g2[:], a["ln2_g"][0:1].partition_broadcast(P).rearrange("p o n -> p (o n)")).then_inc(small, 16)
            sp.dma_start(wr[:, :, 0:GROUPS], a["w_group"][0].rearrange("(k p) n -> p k n", p=P)).then_inc(small, 16)
            sp.dma_start(wr[:, :, GROUPS:LOGITS], a["w_expert"][0].rearrange("(k p) n -> p k n", p=P)).then_inc(small, 16)
            sp.dma_start(rb[:, 0:GROUPS], a["b_group"][0:1].partition_broadcast(P).rearrange("p o n -> p (o n)")).then_inc(small, 16)
            sp.dma_start(rb[:, GROUPS:LOGITS], a["b_expert"][0:1].partition_broadcast(P).rearrange("p o n -> p (o n)")).then_inc(small, 16)
            for kd in range(KD):
                if kd >= 2:
                    sp.wait_ge(wolo, kd - 1)
                sp.dma_start(wo_raw[:, kd % 2], a["w_out"][0, kd * P:(kd + 1) * P, :]).then_inc(wo_in[kd % 2], 16)
            with sp.Fori(0, NT // 2) as i:
                for j in range(2):
                    t = 2 * i + j
                    sp.wait_ge(x1_done, t + 1)
                    sp.dma_start(x[:, j], a["x"][0, bass.ds(t * P, P), :]).then_inc(x_in[j], 16)
                for j in range(2):
                    t = 2 * i + j
                    sp.wait_ge(x1_done, t + 3)
                    sp.dma_start(k["x1_dram"][bass.ds(t * P, P), :], x1[:, j]).then_inc(x1_out[j], 16)
                    sp.wait_ge(h2_done, t + 1)
                    sp.dma_start(k["h2_dram"][bass.ds(t * P, P), :], h2[:, j]).then_inc(h2_out[j], 16)
            for j in range(2):
                sp.wait_ge(x1_out[j], 16 * NT // 2 + 16)
                sp.wait_ge(h2_out[j], 16 * NT // 2 + 16)

        @block.scalar
        def _(act):
            for kd in range(KD):
                act.wait_ge(wo_in[kd % 2], 16 * (kd // 2 + 1))
                act.activation(wo_hi[:, kd], wo_raw[:, kd % 2], ACT.Copy).then_inc(wohi, 1)
            with act.Fori(0, NT // 2) as i:
                for j in range(2):
                    t = 2 * i + j
                    act.wait_ge(mm_done, t + 1)
                    act.activation(cat_hi[:, j], cat[:, :, bass.ds(t * P, P)], ACT.Copy).then_inc(cathi, 1)
                for j in range(2):
                    t = 2 * i + j
                    act.wait_ge(x1_done, t + 3)
                    act.wait_ge(ss_done, t + 1)
                    act.activation(sq[:], x1[:, j], ACT.Square, accum_out=ss[:, j:j + 1]).then_inc(ss_done, 1)
                    act.wait_ge(ss_done, t + 2)
                    act.activation(rms[:, j:j + 1], ss[:, j:j + 1], ACT.Sqrt, bias=k["eps_t"][:],
                                   scale=1.0 / D).then_inc(rms_done, 1)

        @block.vector
        def _(dve):
            dve.sem_inc(x1_done, 2)
            dve.sem_inc(logit_done, 1)
            dve.sem_inc(ss_done, 1)
            for kd in range(KD):
                dve.wait_ge(wohi, kd + 1)
                dve.tensor_tensor(wo_lo[:, kd], wo_raw[:, kd % 2], wo_hi[:, kd].bitcast(F32), ALU.subtract).then_inc(wolo, 1)
            dve.wait_ge(small, 80)

            def logits_out(t):
                for m in range(2):
                    dve.wait_ge(turned, 2 * t + m + 1)
                    dve.tensor_copy(h2T[:, 4 * m:4 * m + 4, :].rearrange("p k n -> p (k n)"), bank(k, 4 + m)).then_inc(h2T_done, 1)
                dve.wait_ge(lg, t + 1)
                dst = logits[:, t, :] if isinstance(t, int) else logits[:, bass.ds(t, 1), :].rearrange("p o n -> p (o n)")
                dve.tensor_tensor(dst, bank(k, 6, LOGITS), rb[:], ALU.add).then_inc(logit_done, 1)

            with dve.Fori(0, NT // 2) as i:
                for j in range(2):
                    t = 2 * i + j
                    dve.wait_ge(cathi, t + 1)
                    dve.tensor_tensor(cat_lo[:, j], cat[:, :, bass.ds(t * P, P)], cat_hi[:, j].bitcast(F32),
                                      ALU.subtract).then_inc(catlo, 1)
                for j in range(2):
                    t = 2 * i + j
                    dve.wait_ge(x_in[j], 16 * i + 16)
                    dve.wait_ge(mm_done, t + 3)
                    dve.wait_ge(x1_out[j], 16 * i + 16)
                    dve.tensor_tensor(x1[:, j], ps[:, 2 * j:2 * j + 2, :].rearrange("p b n -> p (b n)"), x[:, j],
                                      ALU.add).then_inc(x1_done, 1)
                    dve.wait_ge(rms_done, t + 1)
                    dve.reciprocal(inv[:, j:j + 1], rms[:, j:j + 1]).then_inc(inv_done, 1)
                    dve.wait_ge(inv_done, t + 1)
                    dve.wait_ge(h2_out[j], 16 * i + 16)
                    dve.scalar_tensor_tensor(h2[:, j], x1[:, j], inv[:, j:j + 1], g2[:], ALU.mult, ALU.mult).then_inc(h2_done, 1)
                for j in range(2):
                    logits_out(2 * i + j)

        @block.gpsimd
        def _(pool):
            for j in range(2):
                pool.sem_inc(x1_out[j], 16)
                pool.sem_inc(h2_out[j], 16)

        @block.tensor
        def _(pe):
            pe.sem_inc(mm_done, 2)
            with pe.Fori(0, NT // 2) as i:
                for j in range(2):
                    t = 2 * i + j
                    pe.wait_ge(catlo, t + 1)
                    pe.wait_ge(x1_done, t + 1)
                    for hf in range(2):
                        n = 0
                        for kd in range(KD):
                            if hf == 0 and j == 0:
                                pe.wait_ge(wolo, kd + 1)
                            w = slice(hf * HALF, (hf + 1) * HALF)
                            for x_, w_ in ((cat_hi, wo_hi), (cat_lo, wo_hi), (cat_hi, wo_lo)):
                                mm = pe.matmul(bank(k, 2 * j + hf), x_[:, j, kd, :], w_[:, kd, w], start=(n == 0),
                                               stop=(n == 3 * KD - 1))
                                n += 1
                    mm.then_inc(mm_done, 1)
                for j in range(2):
                    t = 2 * i + j
                    pe.wait_ge(h2_done, t + 1)
                    pe.wait_ge(logit_done, t + 1)
                    for m in range(2):
                        for q in range(4):
                            mm = pe.transpose(ps[:, 4 + m, q * P:(q + 1) * P], h2[:, j, (4 * m + q) * P:(4 * m + q + 1) * P],
                                              ident[:])
                        mm.then_inc(turned, 1)
                    pe.wait_ge(h2T_done, 2 * t + 2)
                    for kd in range(KD):
                        mm = pe.matmul(bank(k, 6, LOGITS), h2T[:, kd, :], wr[:, kd, :], start=(kd == 0), stop=(kd == KD - 1))
                    mm.then_inc(lg, 1)


def route(k, c, logits):
    nc, sb, sem, ps, ident, ones, V, A, G = (k[n] for n in ("nc", "sb", "sem", "ps", "ident", "ones", "V", "A", "G"))
    MB = MAX_BLOCKS + 2
    pos = sb("pos", [P, NT, EXPERTS], F32, c)
    pay = sb("pay", [P, NT, EXPERTS, 4], F32, c)
    block_e = sb("block_e", [P, MB], I32, c)
    block_j = sb("block_j", [P, MB], F32, c)
    halves = sb("halves", [P, 1], I32, c)
    tables = (pos, pay, block_e, block_j, halves)
    tmp = ExitStack()
    c = tmp
    JX = -(-T // CAP) - 1
    iota4 = sb("iota4", [P, GROUPS], F32, c)
    iota8 = sb("iota8", [P, PER_GROUP], F32, c)
    tok = sb("tok", [P, NT], F32, c)
    iota_e = sb("iota_e", [P, EXPERTS, JX], F32, c)
    iota_j = sb("iota_j", [P, EXPERTS, JX], F32, c)
    odd = sb("odd", [P, MB // 2 - EXPERTS // 2], F32, c)
    part1 = sb("part1", [P, 1], F32, c)
    before = sb("before", [P, P], F32, c)
    S4 = [P, NT, GROUPS]
    S8 = [P, NT, PER_GROUP]
    S32 = [P, NT, GROUPS, PER_GROUP]
    t4, t4b, og, e4 = (sb(n, S4, F32, c) for n in ("t4", "t4b", "og", "e4"))
    t32v = sb("t32v", [P, NT, PER_GROUP, GROUPS], F32, c)
    sel, t8, o1, o2, pr = (sb(n, S8, F32, c) for n in ("sel", "t8", "o1", "o2", "pr"))
    t32, m1, m2, am = (sb(n, S32, F32, c) for n in ("t32", "m1", "m2", "am"))
    gmax, gsum, cmax, smax, ssum, p1, p2, den, w1, w2_ = (
        sb(n, [P, NT], F32, c) for n in ("gmax", "gsum", "cmax", "smax", "ssum", "p1", "p2", "den", "gw1", "gw2"))
    tot = sb("tot", [P, NT, EXPERTS], F32, c)
    off = sb("off", [P, NT + 1, EXPERTS], F32, c)
    fl, rank, t320 = (sb(n, [P, EXPERTS, JX], F32, c) for n in ("fl", "rank", "t320"))
    ejv = sb("ejv", [P, 4], F32, c)
    diag = sb("diag", [P, 2, P], F32, c)
    made, need_exp, expd, placed, place_mm, ext, ext_mm = (
        sem(n) for n in ("r_made", "r_need", "r_exp", "r_place", "r_placemm", "r_ext", "r_extmm"))

    def over(ap, shape):
        return ap.unsqueeze(len(ap.shape)).to_broadcast(shape)

    with nc.Block() as block:
        @block.gpsimd
        def _(pool):
            iota = dict(allow_small_or_imprecise_dtypes=True)
            pool.iota(iota4[:], [[-1, GROUPS]], base=GROUPS, channel_multiplier=0, **iota).then_inc(made, 1)
            pool.iota(iota8[:], [[-1, PER_GROUP]], base=PER_GROUP, channel_multiplier=0, **iota).then_inc(made, 1)
            pool.iota(tok[:], [[P, NT]], base=0, channel_multiplier=1, **iota).then_inc(made, 1)
            pool.iota(iota_e[:], [[1, EXPERTS], [0, JX]], base=0, channel_multiplier=0, **iota).then_inc(made, 1)
            pool.iota(iota_j[:], [[0, EXPERTS], [1, JX]], base=1, channel_multiplier=0, **iota).then_inc(made, 1)
            pool.iota(part1[:], [[0, 1]], base=1, channel_multiplier=1, **iota).then_inc(made, 1)
            pool.iota(odd[:], [[2, MB // 2 - EXPERTS // 2]], base=1, channel_multiplier=0, **iota).then_inc(made, 1)
            pool.memset(pay[:, :, :, 2:3], 1.0).then_inc(made, 1)
            pool.affine_select(out=before[:], in_=ones[:], compare_op=ALU.is_gt, fill=0.0, base=0,
                               pattern=[[1, P]], channel_multiplier=-1).then_inc(made, 1)

        @block.scalar
        def _(act):
            act.wait_ge(need_exp, 1)
            act.activation(e4[:], t4[:], ACT.Exp).then_inc(expd, 1)
            act.wait_ge(need_exp, 2)
            act.activation(pr[:], t8[:], ACT.Exp).then_inc(expd, 1)

        @block.vector
        def _(dve):
            tt, ts, red = dve.tensor_tensor, dve.tensor_scalar, dve.tensor_reduce
            dve.wait_ge(made, 9)
            gl = logits[:, :, 0:GROUPS]
            el = logits[:, :, GROUPS:LOGITS].rearrange("p t (g j) -> p t j g", g=GROUPS)

            def first_of(hot, vals, top, iota_, shape, tmp_):
                V.step(tt(hot, vals, over(top, shape), ALU.is_ge))
                V.step(tt(tmp_, hot, iota_.unsqueeze(1).to_broadcast(shape), ALU.mult))
                V.step(red(cmax[:], tmp_, X, ALU.max))
                V.step(tt(hot, tmp_, over(cmax[:], shape), ALU.is_equal))

            V.step(red(gmax[:], gl, X, ALU.max))
            V.step(tt(t4[:], gl, over(gmax[:], S4), ALU.subtract))
            dve.sem_inc(need_exp, 1)
            first_of(og[:], gl, gmax[:], iota4[:], S4, t4b[:])
            dve.wait_ge(expd, 1)
            V.step(red(gsum[:], e4[:], X, ALU.add))
            V.step(tt(t32v[:], el, og[:].unsqueeze(2).to_broadcast([P, NT, PER_GROUP, GROUPS]), ALU.mult))
            V.step(red(sel[:], t32v[:], X, ALU.add))
            V.step(red(smax[:], sel[:], X, ALU.max))
            V.step(tt(t8[:], sel[:], over(smax[:], S8), ALU.subtract))
            dve.sem_inc(need_exp, 1)
            dve.wait_ge(expd, 2)
            V.step(red(ssum[:], pr[:], X, ALU.add))
            V.step(dve.reciprocal(ssum[:], ssum[:]))
            V.step(tt(pr[:], pr[:], over(ssum[:], S8), ALU.mult))
            V.step(red(p1[:], pr[:], X, ALU.max))
            first_of(o1[:], pr[:], p1[:], iota8[:], S8, t8[:])
            V.step(dve.scalar_tensor_tensor(sel[:], o1[:], -2.0, pr[:], ALU.mult, ALU.add))
            V.step(red(p2[:], sel[:], X, ALU.max))
            first_of(o2[:], sel[:], p2[:], iota8[:], S8, t8[:])
            V.step(tt(den[:], p1[:], p2[:], ALU.add))
            V.step(tt(den[:], den[:], gsum[:], ALU.mult))
            V.step(dve.reciprocal(den[:], den[:]))
            V.step(tt(w1[:], p1[:], den[:], ALU.mult))
            V.step(tt(w2_[:], p2[:], den[:], ALU.mult))
            ogb = over(og[:], S32)
            V.step(tt(m1[:], ogb, o1[:].unsqueeze(2).to_broadcast(S32), ALU.mult))
            V.step(tt(m2[:], ogb, o2[:].unsqueeze(2).to_broadcast(S32), ALU.mult))
            dve.tensor_tensor(am[:], m1[:], m2[:], ALU.add).then_inc(placed, 1)
            m1f, m2f, amf, t32f = (x[:].rearrange("p t g j -> p t (g j)") for x in (m1, m2, am, t32))
            S = [P, NT, EXPERTS]
            V.step(tt(m1f, m1f, over(w1[:], S), ALU.mult))
            V.step(tt(t32f, m2f, over(w2_[:], S), ALU.mult))
            V.step(tt(pay[:, :, :, 3], m1f, t32f, ALU.add))
            V.step(ts(m2f, m2f, float(T), None, ALU.mult))
            V.step(tt(pay[:, :, :, 1], m2f, over(tok[:], S), ALU.add))
            V.step(dve.tensor_copy(pay[:, :, :, 0], over(tok[:], S)))
            dve.wait_ge(placed, 1)
            dve.wait_ge(place_mm, 1)
            within = bank(k, 0, NT * EXPERTS).rearrange("p (t e) -> p t e", e=EXPERTS)
            V.step(dve.tensor_copy(tot[:].rearrange("p t e -> p (t e)"), bank(k, 1, NT * EXPERTS)))
            V.step(dve.memset(off[:, 0, :], 0.0))
            for t in range(NT):
                V.step(tt(off[:, t + 1, :], off[:, t, :], tot[:, t, :], ALU.add))
            V.step(tt(pos[:], within, off[:, 0:NT, :], ALU.add))
            V.step(ts(pos[:], pos[:], 1.0, None, ALU.add))
            V.step(tt(pos[:], pos[:], amf, ALU.mult))
            V.step(ts(pos[:], pos[:], -1.0, None, ALU.add))
            V.step(ts(fl[:], iota_j[:], float(CAP), None, ALU.mult))
            V.step(tt(fl[:], over(off[:, NT, :], [P, EXPERTS, JX]), fl[:], ALU.is_gt))
            flat = fl[:].rearrange("p e j -> p (e j)")
            V.step(dve.tensor_tensor_scan(rank[:].rearrange("p e j -> p (e j)"), flat, flat, 0.0, ALU.add, ALU.bypass))
            V.step(dve.tensor_copy(cmax[:, 0:1], rank[:, EXPERTS - 1, JX - 1:JX]))
            V.step(tt(rank[:], rank[:], fl[:], ALU.mult))
            V.step(ts(fl[:], rank[:], part1[:, 0:1], None, ALU.is_equal))
            for n, what in enumerate((iota_e, iota_j)):
                V.step(tt(t320[:], fl[:], what[:], ALU.mult))
                V.step(red(ejv[:, n:n + 1], t320[:].rearrange("p e j -> p (e j)"), X, ALU.add))
            V.step(red(ejv[:, 2:3], flat, X, ALU.add))
            V.step(ts(ejv[:, 2:3], ejv[:, 2:3], -2.0 * JX, 2.0 * JX, ALU.mult, ALU.add))
            V.step(tt(ejv[:, 1:2], ejv[:, 1:2], ejv[:, 2:3], ALU.add))
            V.step(ts(ejv[:, 1:2], ejv[:, 1:2], -float(CAP), None, ALU.mult))
            V.step(ts(diag[:, 0, :], ident[:], ejv[:, 0:1], None, ALU.mult))
            dve.tensor_scalar(diag[:, 1, :], ident[:], ejv[:, 1:2], None, ALU.mult).then_inc(ext, 1)
            V.step(dve.tensor_copy(block_e[:, 0:EXPERTS], iota_e[:, :, 0]))
            V.step(dve.memset(block_j[:, 0:EXPERTS], 0.0))
            dve.wait_ge(ext_mm, 1)
            V.step(dve.tensor_copy(block_e[:, EXPERTS:MB], ps[:, 2, 0:MB - EXPERTS]))
            V.step(dve.tensor_copy(block_j[:, EXPERTS:MB], ps[:, 2, P:P + MB - EXPERTS]))
            V.step(ts(odd[:], odd[:], cmax[:, 0:1], None, ALU.is_le))
            V.step(red(cmax[:, 1:2], odd[:], X, ALU.add))
            V.step(ts(halves[:], cmax[:, 1:2], float(EXPERTS // 2), None, ALU.add))

        @block.tensor
        def _(pe):
            pe.wait_ge(made, 9)
            pe.wait_ge(placed, 1)
            am_ = am[:].rearrange("p t g j -> p (t g j)")
            pe.matmul(bank(k, 0, NT * EXPERTS), before[:], am_, start=True, stop=True)
            pe.matmul(bank(k, 1, NT * EXPERTS), ones[:], am_, start=True, stop=True).then_inc(place_mm, 1)
            pe.wait_ge(ext, 1)
            pe.matmul(ps[:, 2, 0:2 * P], ones[:], diag[:].rearrange("p a n -> p (a n)"), start=True, stop=True).then_inc(ext_mm, 1)
    tmp.close()
    return tables


def experts(k, c, tables):
    nc, sb, sem, ps, a, ident, V, A, G = (k[n] for n in ("nc", "sb", "sem", "ps", "a", "ident", "V", "A", "G"))
    pos, pay, block_e, block_j, halves = tables
    MB = MAX_BLOCKS + 2
    w_g = sb("w_g", [P, 2, KD, FF], F32, c)
    w_u = sb("w_u", [P, 2, KD, FF], F32, c)
    w_d = sb("w_d", [P, 2, KF, D], F32, c)
    place = sb("place", [P, CAP], F32, c)
    pos_b = sb("pos_b", [P, NT], F32, c)
    pay_b = sb("pay_b", [P, NT, 4], F32, c)
    hot = sb("hot", [P, NT, CAP], F32, c)
    found = sb("found", [P, 2, 4], F32, c)
    src = sb("src", [P, 1], U32, c)
    far = sb("far", [P, 1], F32, c)
    late_gate = sb("late_gate", [P, 2, 1], F32, c)
    late_far = sb("late_far", [P, 1], F32, c)
    dst = [sb(f"dst{j}", [P, 1], U32, c) for j in range(2)]
    x_g = sb("x_g", [P, D], F32, c)
    x_T = sb("x_T", [P, KD, CAP], F32, c)
    act_g = sb("act_g", [P, KF, CAP], F32, c)
    hid = sb("hid", [P, KF, CAP], F32, c)
    y_T = sb("y_T", [P, KD, CAP], F32, c)
    y = [sb(f"y{j}", [P, D], F32, c) for j in range(2)]
    g_in, u_in, d_in = ([sem(f"e_{n}{j}") for j in range(2)] for n in "gud")
    gathered = sem("e_gathered")
    scattered = [sem(f"e_scattered{j}") for j in range(2)]
    names = "e_made e_posb e_hot e_found_mm e_found e_src e_turn e_xT e_g e_u e_sig e_gated e_hid e_d e_yT e_yturn " \
            "e_y e_late e_passed".split()
    (made, posb_done, hot_done, found_mm, found_done, src_done, turned, xT_done, g_done, u_done, sig_done, gated,
     hid_done, d_done, yT_done, yturned, y_done, late, passed) = (sem(n) for n in names)
    wg, wu, wd = (a[n][0] for n in ("exp_w_gate", "exp_w_up", "exp_w_down"))

    with nc.Block() as block:
        @block.sync
        def _(sp):
            for j in range(2):
                for w, src_w, w_in in ((w_g, wg, g_in), (w_u, wu, u_in), (w_d, wd, d_in)):
                    sp.dma_start(w[:, j], src_w[j].rearrange("(k p) n -> p k n", p=P)).then_inc(w_in[j], 16)
            n2 = sp.value_load(halves[0:1, 0:1], min_val=EXPERTS // 2, max_val=MB // 2)
            with sp.Fori(1, n2) as i:
                for j in range(2):
                    b = 2 * i + j
                    e = sp.value_load(block_e[0:1, bass.ds(b, 1)], min_val=0, max_val=EXPERTS - 1)
                    g, u, d = (w[bass.ds(e, 1)].rearrange("o (k p) n -> p (o k) n", p=P) for w in (wg, wu, wd))
                    sp.wait_ge(g_done, b - 1)
                    sp.dma_start(w_g[:, j], g).then_inc(g_in[j], 16)
                    sp.wait_ge(u_done, b)
                    sp.dma_start(w_u[:, j], u).then_inc(u_in[j], 16)
                    sp.wait_ge(d_done, b - 1)
                    sp.dma_start(w_d[:, j], d).then_inc(d_in[j], 16)

        @block.gpsimd
        def _(pool):
            pool.iota(place[:], [[1, CAP]], base=0, channel_multiplier=0,
                      allow_small_or_imprecise_dtypes=True).then_inc(made, 1)
            pool.memset(x_g[:], 0.0).then_inc(made, 1)
            pool.memset(y_T[:], 0.0).then_inc(made, 1)
            pool.memset(late_gate[:], 0.0).then_inc(made, 1)
            for j in range(2):
                pool.memset(dst[j][:], 2 * T).then_inc(made, 1)
                pool.memset(y[j][:], 0.0).then_inc(made, 1)
            pool.wait_ge(made, 8)

            def gather(b):
                pool.wait_ge(src_done, b + 1)
                pool.wait_ge(turned, b + 1)
                pool.sem_inc(passed, 1)
                pool.indirect_dma_start(x_g[0:CAP, :], None, k["h2_dram"][:, :],
                                        bass.IndirectOffsetOnAxis(ap=src[0:CAP, :], axis=0),
                                        bounds_check=T - 1, oob_is_err=False).then_inc(gathered, 16)

            def scatter(b, j):
                pool.wait_ge(y_done, b + 2)
                pool.wait_ge(late, 3 * b + 1)
                pool.sem_inc(passed, 1)
                pool.indirect_dma_start(k["y2_dram"][:, :], bass.IndirectOffsetOnAxis(ap=dst[j][0:CAP, :], axis=0),
                                        y[j][0:CAP, :], None, bounds_check=2 * T - 1,
                                        oob_is_err=False).then_inc(scattered[j], 16)

            for j in range(2):
                pool.indirect_dma_start(k["y2_dram"][:, :], bass.IndirectOffsetOnAxis(ap=dst[j][0:CAP, :], axis=0),
                                        y[j][0:CAP, :], None, bounds_check=2 * T - 1,
                                        oob_is_err=False).then_inc(scattered[j], 16)
            gather(0)
            n2 = pool.value_load(halves[0:1, 0:1], min_val=EXPERTS // 2, max_val=MB // 2)
            with pool.Fori(0, n2) as i:
                for j in range(2):
                    gather(2 * i + j + 1)
                    scatter(2 * i + j, 1 - j)
            scatter(2 * n2, 1)
            pool.wait_ge(scattered[0], 16 * n2 + 16)
            pool.wait_ge(scattered[1], 16 * n2 + 32)
            pool.wait_ge(gathered, 32 * n2 + 16)

        @block.scalar
        def _(act):
            act.wait_ge(made, 8)

            def x_out(b):
                act.wait_ge(turned, b + 2)
                act.wait_ge(u_done, b + 1)
                act.activation(x_T[:].rearrange("p (a k) n -> p a (k n)", a=2), ps[:, 4:6, 0:4 * CAP],
                               ACT.Copy).then_inc(xT_done, 1)

            def y_out(b, i, j):
                act.wait_ge(yturned, b + 1)
                act.wait_ge(late, 3 * b + 1)
                act.wait_ge(scattered[j], 16 * i + 16)
                act.activation(y[j][0:CAP, :], ps[0:CAP, 6:8, :].rearrange("p b n -> p (b n)"), ACT.Copy,
                               scale=late_gate[0:CAP, j, :]).then_inc(y_done, 1)

            x_out(0)
            n2 = act.value_load(halves[0:1, 0:1], min_val=EXPERTS // 2, max_val=MB // 2)
            with act.Fori(0, n2) as i:
                for j in range(2):
                    b = 2 * i + j
                    act.wait_ge(g_done, b + 1)
                    act.wait_ge(hid_done, b + 1)
                    act.activation(act_g[:].rearrange("p k n -> p (k n)"), bank(k, 0, KF * CAP), ACT.Sigmoid)\
                       .then_inc(sig_done, 1)
                    y_out(b, i, 1 - j)
                    x_out(b + 1)
                    act.wait_ge(d_done, b + 1)
                    act.activation(y_T[:].rearrange("p (a k) n -> p a (k n)", a=2), ps[:, 2:4, 0:4 * CAP],
                                   ACT.Copy).then_inc(yT_done, 1)
            y_out(2 * n2, n2, 1)

        @block.vector
        def _(dve):
            dve.sem_inc(hid_done, 1)
            dve.sem_inc(late, 1)
            dve.wait_ge(made, 8)

            def find(b, e):
                dve.wait_ge(found_mm, b + 1)
                dve.tensor_copy(pay_b[:], pay[:, :, bass.ds(e, 1), :].rearrange("p t o n -> p t (o n)"))\
                   .then_inc(posb_done, 1)
                dve.tensor_scalar(pos_b[:], pos[:, :, bass.ds(e, 1)].rearrange("p t o -> p (t o)"),
                                  block_j[:, bass.ds(b, 1)], None, ALU.add).then_inc(posb_done, 1)
                dve.wait_ge(posb_done, 2 * b + 2)
                for t in range(NT):
                    ins = dve.tensor_scalar(hot[:, t, :], place[:], pos_b[:, t:t + 1], None, ALU.is_equal)
                ins.then_inc(hot_done, 1)

            def found_out(b, j, first=False):
                dve.wait_ge(found_mm, b + 2)
                dve.tensor_copy(found[0:CAP, j, :], ps[0:CAP, 4, 4 * CAP:4 * CAP + 4]).then_inc(found_done, 1)
                dve.wait_ge(found_done, 2 * b + 1)
                dve.tensor_scalar(far[0:CAP], found[0:CAP, j, 2:3], -FAR, FAR, ALU.mult, ALU.add).then_inc(found_done, 1)
                dve.wait_ge(found_done, 2 * b + 2)
                if not first:
                    dve.wait_ge(gathered, 16 * b)
                dve.tensor_tensor(src[0:CAP], found[0:CAP, j, 0:1], far[0:CAP], ALU.add).then_inc(src_done, 1)
                dve.wait_ge(src_done, b + 1)

            find(0, 0)
            found_out(0, 0, first=True)
            n2 = dve.value_load(halves[0:1, 0:1], min_val=EXPERTS // 2, max_val=MB // 2)
            with dve.Fori(0, n2) as i:
                for j in range(2):
                    b = 2 * i + j
                    e = dve.value_load(block_e[0:1, bass.ds(b + 1, 1)], min_val=0, max_val=EXPERTS - 1)
                    find(b + 1, e)
                    found_out(b + 1, 1 - j)
                    dve.wait_ge(sig_done, b + 1)
                    dve.tensor_tensor(hid[:].rearrange("p k n -> p (k n)"), bank(k, 0, KF * CAP),
                                      act_g[:].rearrange("p k n -> p (k n)"), ALU.mult).then_inc(gated, 1)
                    dve.wait_ge(u_done, b + 2)
                    dve.wait_ge(gated, b + 1)
                    dve.tensor_tensor(hid[:].rearrange("p k n -> p (k n)"), bank(k, 1, KF * CAP),
                                      hid[:].rearrange("p k n -> p (k n)"), ALU.mult).then_inc(hid_done, 1)
                    dve.wait_ge(y_done, b + 1)
                    dve.wait_ge(scattered[j], 16 * i + 16 + 16 * j)
                    dve.tensor_copy(late_gate[0:CAP, j, :], found[0:CAP, j, 3:4]).then_inc(late, 1)
                    dve.tensor_scalar(late_far[0:CAP], found[0:CAP, j, 2:3], -FAR, FAR, ALU.mult, ALU.add).then_inc(late, 1)
                    dve.wait_ge(late, 3 * b + 3)
                    dve.tensor_tensor(dst[j][0:CAP], found[0:CAP, j, 1:2], late_far[0:CAP], ALU.add).then_inc(late, 1)
                    dve.wait_ge(late, 3 * b + 4)

        @block.tensor
        def _(pe):
            pe.sem_inc(found_mm, 1)
            pe.sem_inc(turned, 1)
            pe.sem_inc(u_done, 1)
            pe.sem_inc(yT_done, 1)
            pe.sem_inc(y_done, 1)
            pe.wait_ge(made, 8)

            def find(b):
                pe.wait_ge(hot_done, b + 1)
                for t in range(NT):
                    mm = pe.matmul(ps[0:CAP, 4, 4 * CAP:4 * CAP + 4], hot[:, t, :], pay_b[:, t, :], start=(t == 0),
                                   stop=(t == NT - 1))
                mm.then_inc(found_mm, 1)

            def turn_x(b):
                pe.wait_ge(gathered, 16 * b + 16)
                pe.wait_ge(found_done, 2 * b + 1)
                for kd in range(KD):
                    mm = pe.transpose(ps[:, 4 + kd // 4, (kd % 4) * CAP:(kd % 4 + 1) * CAP],
                                      x_g[0:CAP, kd * P:(kd + 1) * P], ident[0:CAP, 0:CAP])
                mm.then_inc(turned, 1)

            def turn_y(b):
                pe.wait_ge(yT_done, b + 1)
                pe.wait_ge(y_done, b + 1)
                for kd in range(KD):
                    mm = pe.transpose(ps[0:CAP, 6 + kd // 4, (kd % 4) * P:(kd % 4 + 1) * P], y_T[:, kd, :], ident[:])
                mm.then_inc(yturned, 1)

            find(0)
            turn_x(0)
            n2 = pe.value_load(halves[0:1, 0:1], min_val=EXPERTS // 2, max_val=MB // 2)
            with pe.Fori(0, n2) as i:
                for j in range(2):
                    b = 2 * i + j
                    pe.wait_ge(xT_done, b + 1)
                    find(b + 1)
                    for w, w_in, o, done in ((w_g, g_in, 0, g_done), (w_u, u_in, 1, u_done)):
                        pe.wait_ge(w_in[j], 16 * i + 16)
                        pe.wait_ge(hid_done, b + 1)
                        for f in range(KF):
                            for kd in range(KD):
                                mm = pe.matmul(ps[:, o, f * CAP:(f + 1) * CAP], w[:, j, kd, f * P:(f + 1) * P],
                                               x_T[:, kd, :], start=(kd == 0), stop=(kd == KD - 1))
                        mm.then_inc(done, 1)
                    turn_y(b)
                    turn_x(b + 1)
                    pe.wait_ge(d_in[j], 16 * i + 16)
                    pe.wait_ge(hid_done, b + 2)
                    for m in range(KD):
                        for f in range(KF):
                            mm = pe.matmul(ps[:, 2 + m // 4, (m % 4) * CAP:(m % 4 + 1) * CAP], w_d[:, j, f, m * P:(m + 1) * P],
                                           hid[:, f, :], start=(f == 0), stop=(f == KF - 1))
                    mm.then_inc(d_done, 1)
            turn_y(2 * n2)


def combine(k, c):
    nc, sb, sem, a = (k[n] for n in ("nc", "sb", "sem", "a"))
    B = 4
    x1 = sb("c_x1", [P, B, D], F32, c)
    ya = sb("c_ya", [P, B, D], F32, c)
    yb = sb("c_yb", [P, B, D], F32, c)
    sq = sb("c_sq", [P, D], F32, c)
    gf = sb("gf", [P, D], F32, c)
    ss, rms, inv = (sb(n, [P, B], F32, c) for n in ("c_ss", "c_rms", "c_inv"))
    x_in, a_in, b_in, out_s = ([sem(f"c_{n}{j}") for j in range(B)] for n in "xabo")
    small, sum1, sum2, ssd, rmsd, invd, od = (sem(f"c_{n}") for n in ("small", "sum1", "sum2", "ss", "rms", "inv", "out"))
    with nc.Block() as block:
        @block.sync
        def _(sp):
            sp.dma_start(gf[:], a["ln_f_g"].rearrange("(o n) -> o n", o=1).partition_broadcast(P).rearrange("p o n -> p (o n)"))\
              .then_inc(small, 16)
            for t in range(NT):
                j = t % B
                if t >= B:
                    sp.wait_ge(out_s[j], 16)
                    sp.wait_ge(sum2, t - B + 1)
                sp.dma_start(x1[:, j], k["x1_dram"][t * P:(t + 1) * P, :]).then_inc(x_in[j], 16)
                sp.dma_start(ya[:, j], k["y2_dram"][t * P:(t + 1) * P, :]).then_inc(a_in[j], 16)
                sp.dma_start(yb[:, j], k["y2_dram"][T + t * P:T + (t + 1) * P, :]).then_inc(b_in[j], 16)

        @block.vector
        def _(dve):
            dve.wait_ge(small, 16)
            for t in range(NT):
                j = t % B
                dve.wait_ge(x_in[j], 16 * (t // B + 1))
                dve.wait_ge(a_in[j], 16 * (t // B + 1))
                dve.wait_ge(b_in[j], 16 * (t // B + 1))
                dve.tensor_tensor(ya[:, j], ya[:, j], yb[:, j], ALU.add).then_inc(sum1, 1)
                dve.wait_ge(sum1, t + 1)
                dve.tensor_tensor(x1[:, j], x1[:, j], ya[:, j], ALU.add).then_inc(sum2, 1)
                dve.wait_ge(rmsd, t + 1)
                dve.reciprocal(inv[:, j:j + 1], rms[:, j:j + 1]).then_inc(invd, 1)
                dve.wait_ge(invd, t + 1)
                dve.scalar_tensor_tensor(ya[:, j], x1[:, j], inv[:, j:j + 1], gf[:], ALU.mult, ALU.mult).then_inc(od, 1)

        @block.scalar
        def _(act):
            for t in range(NT):
                j = t % B
                act.wait_ge(sum2, t + 1)
                if t >= 1:
                    act.wait_ge(ssd, t)
                act.activation(sq[:], x1[:, j], ACT.Square, accum_out=ss[:, j:j + 1]).then_inc(ssd, 1)
                act.wait_ge(ssd, t + 1)
                act.activation(rms[:, j:j + 1], ss[:, j:j + 1], ACT.Sqrt, bias=k["eps_t"][:], scale=1.0 / D).then_inc(rmsd, 1)

        @block.gpsimd
        def _(pool):
            for t in range(NT):
                pool.wait_ge(od, t + 1)
                pool.dma_start(a["out"][0, t * P:(t + 1) * P, :], ya[:, t % B]).then_inc(out_s[t % B], 16)
            for j in range(B):
                pool.wait_ge(out_s[j], 16 * NT // B)


def kernel(**inputs):
    import concourse.bacc as bacc
    from concourse.bass_utils import run_bass_kernel_spmd

    nc = bacc.Bacc("TRN2", target_bir_lowering=False, num_devices=1)
    arrays, args = {}, {}
    for name, value in inputs.items():
        arr = np.ascontiguousarray(value)
        arrays[name] = arr
        args[name] = nc.dram_tensor(name, arr.shape, mybir.dt.from_np(arr.dtype), kind="ExternalInput").ap()
    args["out"] = nc.dram_tensor("out", (1, T, D), F32, kind="ExternalOutput").ap()
    build(nc, args)
    r = run_bass_kernel_spmd(nc, [arrays], core_ids=[0])
    return r.results[0]["out"]
```

```python
from contextlib import ExitStack

import numpy as np

import concourse.bass as bass
from concourse import mybir

F32 = mybir.dt.float32
F32R = mybir.dt.float32r
I32 = mybir.dt.int32
U32 = mybir.dt.uint32
ALU = mybir.AluOpType
ACT = mybir.ActivationFunctionType
X = mybir.AxisListType.X

P = 128
T = 1024
D = 1024
NT = T // P
KD = D // P
HALF = 512
NH = T // HALF
SB_HEADS, SB_DIM = 8, 64
SB_PAIRS = SB_HEADS // 2
SB_W = SB_HEADS * SB_DIM
GLA_HEADS, DK, DV = 4, 64, 128
GLA_PAIRS = GLA_HEADS // 2
KW, VW = GLA_HEADS * DK, GLA_HEADS * DV
RANK = 16
TAU = 16.0
D_IN = 3 * SB_W + 2 * KW + 2 * VW + RANK
COL_SB_Q, COL_SB_K, COL_SB_V = 0, SB_W, 2 * SB_W
COL_G_Q = 3 * SB_W
COL_G_K = COL_G_Q + KW
COL_G_V = COL_G_K + KW
COL_G_R = COL_G_V + VW
COL_LR = D_IN - P
LEVELS = 7
GROUPS, PER_GROUP = 4, 8
EXPERTS = GROUPS * PER_GROUP
LOGITS = GROUPS + EXPERTS
FF = 512
KF = FF // P
CAP = 96
MAX_BLOCKS = EXPERTS + 2 * T // (CAP + 1)
MAX_HALVES = (MAX_BLOCKS + 1) // 2
EPS = 1e-6
SCALE = SB_DIM ** -0.5
FAR = 4096.0


class Chain:

    def __init__(self, eng, sem):
        self.eng, self.sem, self.at, self.n = eng, sem, 0, 0

    def mark(self, ins):
        ins.then_inc(self.sem, 1)
        self.n += 1

    def join(self):
        self.eng.wait_ge(self.sem, self.at + self.n)

    def step(self, ins):
        self.mark(ins)
        self.join()

    def enter(self, i, per):
        base = self.at + self.n
        self.at, self.n = base + i * per, 0
        return base

    def leave(self, base, per, times):
        assert self.n == per, (self.n, per)
        self.at, self.n = base + per * times, 0


def build(nc, a):
    with ExitStack() as ctx:
        _build(nc, ctx, a)


def _build(nc, ctx, a):
    def sb(name, shape, dt=F32, c=ctx):
        return c.enter_context(nc.sbuf_tensor(name, shape, dt))

    def sem(name, c=None):
        return ctx.enter_context(nc.semaphore(name))

    def dram(name, shape):
        return nc.dram_tensor(name, shape, F32)

    ps = ctx.enter_context(nc.psum_tensor("ps", [P, 8, HALF], F32))

    x1_dram = dram("x1_dram", [T, D])
    h2_dram = dram("h2_dram", [T, D])
    y2_dram = dram("y2_dram", [2 * T, D])

    ident = sb("ident", [P, P])
    ones = sb("ones", [P, P])
    eps_t = sb("eps_t", [P, 1])

    chain_v = sem("chain_v")
    chain_g = sem("chain_g")
    chain_a = sem("chain_a")
    made = sem("made")
    V = Chain(nc.vector, chain_v)
    G = Chain(nc.gpsimd, chain_g)
    A = Chain(nc.scalar, chain_a)
    k = dict(nc=nc, sb=sb, sem=sem, ps=ps, a=a, ident=ident, ones=ones, eps_t=eps_t, V=V, G=G, A=A,
             x1_dram=x1_dram, h2_dram=h2_dram, y2_dram=y2_dram)

    with nc.Block() as block:
        @block.gpsimd
        def _(pool):
            G.step(pool.memset(ident[:], 0.0))
            pool.affine_select(out=ident[:], in_=ident[:], compare_op=ALU.not_equal, fill=1.0, base=0,
                               pattern=[[-1, P]], channel_multiplier=1).then_inc(made, 1)
            pool.memset(ones[:], 1.0).then_inc(made, 1)
            pool.memset(eps_t[:], EPS).then_inc(made, 1)
            pool.wait_ge(made, 3)

    logits = sb("logits", [P, NT, LOGITS])
    with ExitStack() as c:
        cat = sb("cat", [P, KD, T], F32, c)
        with ExitStack() as front:
            h_hi = sb("h_hi", [P, KD, T], F32R, front)
            h_lo = sb("h_lo", [P, KD, T], F32R, front)
            with ExitStack() as c1:
                w_raw = sb("w_raw", [P, 3, KD, P], F32, c1)
                w_in = [sem(f"sbw_in{j}") for j in range(3)]
                with ExitStack() as c2:
                    norm_and_turn(k, c2, h_hi, h_lo, w_raw, w_in)
                with ExitStack() as c2:
                    stick_breaking(k, c2, h_hi, h_lo, cat, w_raw, w_in)
            with ExitStack() as c2:
                linear_attention(k, c2, h_hi, h_lo, cat)
        mix_out(k, c, cat, logits)
    with ExitStack() as c:
        w = expert_weights(k, c)
        tables = route(k, c, logits, w)
        experts(k, c, tables, w)
    with ExitStack() as c:
        combine(k, c)


def bank(k, i, n=HALF, p=P):
    return k["ps"][0:p, i, 0:n]


def norm_and_turn(k, c, h_hi, h_lo, w_raw, w_in):
    nc, sb, sem, a, ident, V, A = (k[n] for n in ("nc", "sb", "sem", "a", "ident", "V", "A"))
    xt = sb("xt", [P, NT, D], F32, c)
    xn = sb("xn", [P, NT, D], F32, c)
    squares = sb("squares", [P, D], F32, c)
    ss = sb("ss", [P, NT], F32, c)
    rms = sb("rms", [P, NT], F32, c)
    inv = sb("inv", [P, NT], F32, c)
    g1 = sb("g1", [P, KD], F32, c)
    x_in = [sem(f"x_in{t}", c) for t in range(NT)]
    g_in = sem("g_in", c)
    rms_done, xn_done = sem("rms_done", c), sem("xn_done", c)
    turned, hi_done, lo_done = sem("turned", c), sem("hi_done", c), sem("lo_done", c)
    groups = [(hf, kd) for hf in range(NH) for kd in range(KD)]
    per = NT // NH
    with nc.Block() as block:
        @block.sync
        def _(sp):
            for t in range(NT):
                sp.dma_start(xt[:, t, :], a["x"][0, t * P:(t + 1) * P, :]).then_inc(x_in[t], 16)
            with nc.allow_non_contiguous_dma(reason="a thousand gains, features to partitions"):
                sp.dma_start(g1[:], a["ln1_g"][0].rearrange("(k p) -> p k", p=P)).then_inc(g_in, 16)
            for j, col in enumerate((COL_SB_Q, COL_SB_K, COL_SB_V)):
                sp.dma_start(w_raw[:, j], a["w_in"][0, :, col:col + P].rearrange("(k p) c -> p k c", p=P))\
                  .then_inc(w_in[j], 16)

        @block.scalar
        def _(act):
            for t in range(NT):
                act.wait_ge(x_in[t], 16)
                A.step(act.activation(squares[:], xt[:, t, :], ACT.Square, accum_out=ss[:, t:t + 1]))
                if t % per == per - 1:
                    part = slice(t + 1 - per, t + 1)
                    act.activation(rms[:, part], ss[:, part], ACT.Sqrt, bias=k["eps_t"][:], scale=1.0 / D).then_inc(rms_done, 1)
            act.wait_ge(g_in, 16)
            for n, (hf, kd) in enumerate(groups):
                act.wait_ge(turned, n + 1)
                act.activation(h_hi[:, kd, hf * HALF:(hf + 1) * HALF], bank(k, n % 4), ACT.Copy,
                               scale=g1[:, kd:kd + 1]).then_inc(hi_done, 1)

        @block.vector
        def _(dve):
            for t in range(NT):
                if t % per == 0:
                    dve.wait_ge(rms_done, t // per + 1)
                    V.step(dve.reciprocal(inv[:, t:t + per], rms[:, t:t + per]))
                dve.tensor_scalar(xn[:, t, :], xt[:, t, :], inv[:, t:t + 1], None, ALU.mult).then_inc(xn_done, 1)
            dve.wait_ge(g_in, 16)
            for n, (hf, kd) in enumerate(groups):
                dve.wait_ge(hi_done, n + 1)
                cols = slice(hf * HALF, (hf + 1) * HALF)
                dve.scalar_tensor_tensor(h_lo[:, kd, cols], bank(k, n % 4), g1[:, kd:kd + 1],
                                         h_hi[:, kd, cols].bitcast(F32), ALU.mult,
                                         ALU.subtract).then_inc(lo_done, 1)

        @block.tensor
        def _(pe):
            for n, (hf, kd) in enumerate(groups):
                if kd == 0:
                    pe.wait_ge(xn_done, per * (hf + 1))
                if n >= 4:
                    pe.wait_ge(lo_done, n - 3)
                for j in range(per):
                    mm = pe.transpose(k["ps"][:, n % 4, j * P:(j + 1) * P],
                                      xn[:, hf * per + j, kd * P:(kd + 1) * P], ident[:])
                mm.then_inc(turned, 1)


def project(pe, k, w_hi, w_lo, h_hi, h_lo, half, out):
    cols = slice(half * HALF, (half + 1) * HALF)
    n = 0
    for kd in range(KD):
        for w, h in ((w_hi, h_hi), (w_hi, h_lo), (w_lo, h_hi)):
            mm = pe.matmul(out, w[:, kd, :], h[:, kd, cols], start=(n == 0), stop=(n == 3 * KD - 1))
            n += 1
    return mm


def stick_breaking(k, c, h_hi, h_lo, cat, w_raw, w_in_s):
    nc, sb, sem, ps, a, ident = (k[n] for n in ("nc", "sb", "sem", "ps", "a", "ident"))
    w_hi = sb("w_hi", [P, 3, KD, P], F32R, c)
    w_lo = sb("w_lo", [P, 3, KD, P], F32R, c)
    q_hi, q_lo = (sb(n, [P, 2, T], F32R, c) for n in ("q_hi", "q_lo"))
    k_hi, k_lo = (sb(n, [P, T], F32R, c) for n in ("k_hi", "k_lo"))
    v_f = sb("v_f", [P, T], F32, c)
    v = sb("v", [P, 2, NT, P], F32, c)
    stay = sb("stay", [P, 2, T], F32, c)
    beta = sb("beta", [P, 2, T], F32, c)
    prod = sb("prod", [P, 2, T + 1], F32, c)
    wT = sb("wT", [P, 2, T], F32, c)
    names = "sb_hi sb_lo sb_proj sb_qkv sb_vturn sb_v sb_z sb_sig sb_masked " \
            "sb_scan sb_w sb_wturn sb_wT sb_pv sb_cat sb_one sb_qklo sb_passed".split()
    (hi_done, lo_done, projd, qkv_done, vturn, v_done, z_done, sig_done, masked,
     scan_done, w_done, wturn, wT_done, pv_done, cat_done, one, qk_lo, passed) = (sem(n, c) for n in names)
    U = 2 * NT
    units = [(i, h) for i in (*range(1, NT, 2), *range(NT - 2, -1, -2)) for h in range(2)]
    nturn = [(i + 4) // 4 for i, h in units]
    before = [sum(nturn[:u]) for u in range(U)]
    TURNS = sum(nturn)
    SPLIT_AT = 10
    w_dram = a["w_in"][0].rearrange("(k p) c -> p k c", p=P)
    col0 = (COL_SB_Q, COL_SB_K, COL_SB_V)

    def nk(i):
        return (i + 1) * P

    def split_hi(act, p, j):
        act.wait_ge(w_in_s[j], 16 * p + 16)
        act.wait_ge(projd, 6 * p + 2 * j + 2)
        act.activation(w_hi[:, j], w_raw[:, j], ACT.Copy).then_inc(hi_done, 1)

    def split_lo(dve, p, j):
        dve.wait_ge(hi_done, 3 * p + j + 1)
        dve.tensor_tensor(w_lo[:, j], w_raw[:, j], w_hi[:, j].bitcast(F32), ALU.subtract).then_inc(lo_done, 1)

    with nc.Block() as block:
        @block.sync
        def _(sp):
            with sp.Fori(1, SB_PAIRS) as p:
                for j in range(3):
                    sp.wait_ge(lo_done, 3 * p + j + 1)
                    sp.dma_start(w_raw[:, j], w_dram[:, :, bass.ds(p * P + col0[j], P)]).then_inc(w_in_s[j], 16)
            for j in range(3):
                sp.wait_ge(lo_done, 3 * SB_PAIRS + j + 1)
                sp.dma_start(w_raw[0:1, j, 0, :], w_dram[0:1, 0, 0:P]).then_inc(w_in_s[j], 16)

        @block.scalar
        def _(act):
            for j in range(3):
                split_hi(act, 0, j)
            with act.Fori(0, SB_PAIRS) as p:
                act.wait_ge(one, 4)
                for n in range(6):
                    act.wait_ge(projd, 6 * p + n + 7)
                    j, hf = divmod(n, 2)
                    cols = slice(hf * HALF, (hf + 1) * HALF)
                    if j == 0:
                        for h in range(2):
                            rows = slice(SB_DIM * h, SB_DIM * (h + 1))
                            ins = act.activation(q_hi[rows, h, cols], bank(k, n % 4)[rows], ACT.Copy)
                    else:
                        ins = act.activation((k_hi if j == 1 else v_f)[:, cols], bank(k, n % 4), ACT.Copy)
                    ins.then_inc(qkv_done, 1)
                for u, (i, h) in enumerate(units):
                    act.wait_ge(z_done, U * p + u + 1)
                    act.wait_ge(w_done, U * p + u + 1)
                    z = ps[:, 2 * (u % 2):2 * (u % 2) + 2, :].rearrange("p b n -> p (b n)")[:, 0:nk(i)]
                    act.activation(stay[:, u % 2, 0:nk(i)], z, ACT.Sigmoid, scale=-SCALE).then_inc(sig_done, 1)
                    act.wait_ge(wturn, TURNS * p + 4 + (before[u - 1] if u else -nturn[U - 1]))
                    act.activation(beta[:, u % 2, 0:nk(i)], z, ACT.Sigmoid, scale=SCALE).then_inc(sig_done, 1)
                    if SPLIT_AT <= u < SPLIT_AT + 3:
                        split_hi(act, p + 1, u - SPLIT_AT)

        @block.gpsimd
        def _(pool):
            pool.memset(q_hi[:].bitcast(F32), 0.0).then_inc(one, 1)
            pool.memset(q_lo[:].bitcast(F32), 0.0).then_inc(one, 1)
            pool.memset(v[:], 0.0).then_inc(one, 1)
            pool.memset(prod[:, :, T:T + 1], 1.0).then_inc(one, 1)
            fill_one, fill_zero = pool.to_reg(1.0), pool.to_reg(0.0)
            pool.sem_inc(w_done, 2)
            with pool.Fori(0, SB_PAIRS) as p:
                for u, (i, h) in enumerate(units):
                    b = u % 2
                    diag = slice(i * P, (i + 1) * P)
                    pool.wait_ge(sig_done, 2 * U * p + 2 * u + 1)
                    pool.sem_inc(passed, 1)
                    pool.affine_select(out=stay[:, b, diag], in_=stay[:, b, diag], compare_op=ALU.is_gt,
                                       fill=fill_one, base=0, pattern=[[-1, P]], channel_multiplier=1).then_inc(masked, 1)
                    pool.wait_ge(sig_done, 2 * U * p + 2 * u + 2)
                    pool.sem_inc(passed, 1)
                    pool.affine_select(out=beta[:, b, diag], in_=beta[:, b, diag], compare_op=ALU.is_gt,
                                       fill=fill_zero, base=0, pattern=[[-1, P]], channel_multiplier=1).then_inc(masked, 1)
                    pool.wait_ge(masked, 2 * U * p + 2 * u + 2)
                    pool.wait_ge(scan_done, U * p + u + 1)
                    pool.tensor_tensor(beta[:, b, 0:nk(i)], beta[:, b, 0:nk(i)], prod[:, b, T + 1 - nk(i):T + 1],
                                       ALU.mult).then_inc(w_done, 1)

        @block.vector
        def _(dve):
            dve.sem_inc(lo_done, 3)
            dve.sem_inc(cat_done, 2)
            for j in range(3):
                split_lo(dve, 0, j)
            with dve.Fori(0, SB_PAIRS) as p:
                dve.wait_ge(one, 4)
                for n in range(4):
                    dve.wait_ge(qkv_done, 6 * p + n + 1)
                    j, hf = divmod(n, 2)
                    cols = slice(hf * HALF, (hf + 1) * HALF)
                    if j == 0:
                        for h in range(2):
                            rows = slice(SB_DIM * h, SB_DIM * (h + 1))
                            ins = dve.tensor_tensor(q_lo[rows, h, cols], bank(k, n % 4)[rows],
                                                    q_hi[rows, h, cols].bitcast(F32), ALU.subtract)
                    else:
                        ins = dve.tensor_tensor(k_lo[:, cols], bank(k, n % 4), k_hi[:, cols].bitcast(F32), ALU.subtract)
                    ins.then_inc(qk_lo, 1)
                for n in range(2):
                    dve.wait_ge(vturn, 2 * p + n + 1)
                    for h in range(2):
                        dims = slice(SB_DIM * h, SB_DIM * (h + 1))
                        ins = dve.tensor_copy(v[:, h, 4 * n:4 * n + 4, dims],
                                              bank(k, 4 + n).rearrange("p (t n) -> p t n", n=P)[:, :, dims])
                    ins.then_inc(v_done, 1)
                for u in range(U + 1):
                    if SPLIT_AT < u <= SPLIT_AT + 3:
                        split_lo(dve, p + 1, u - SPLIT_AT - 1)
                    if u < U:
                        i, h = units[u]
                        dve.wait_ge(masked, 2 * U * p + 2 * u + 1)
                        dve.wait_ge(w_done, U * p + u + 1)
                        dve.tensor_tensor_scan(prod[:, u % 2, T - nk(i):T][:, ::-1], stay[:, u % 2, 0:nk(i)][:, ::-1],
                                               stay[:, u % 2, 0:nk(i)][:, ::-1], 1.0, ALU.mult,
                                               ALU.bypass).then_inc(scan_done, 1)
                    if u >= 1:
                        i, h = units[u - 1]
                        for m in range(nturn[u - 1]):
                            w0, w1 = 4 * P * m, min(4 * P * (m + 1), nk(i))
                            n = before[u - 1] + m
                            dve.wait_ge(wturn, TURNS * p + n + 1 + 4)
                            dve.wait_ge(pv_done, U * p + u)
                            dve.tensor_copy(wT[:, (u - 1) % 2, w0:w1], bank(k, 4 + n % 2, w1 - w0)).then_inc(wT_done, 1)
                for n in range(2):
                    dve.wait_ge(pv_done, U * p + U + 2)
                    dve.tensor_copy(cat[:, bass.ds(p, 1), n * HALF:(n + 1) * HALF].rearrange("p o n -> p (o n)"),
                                    bank(k, 6 + n)).then_inc(cat_done, 1)

        @block.tensor
        def _(pe):
            pe.sem_inc(projd, 6)
            pe.sem_inc(pv_done, 2)
            pe.sem_inc(wturn, 4)
            with pe.Fori(0, SB_PAIRS) as p:
                for n in range(6):
                    j, hf = divmod(n, 2)
                    if hf == 0:
                        pe.wait_ge(lo_done, 3 * p + j + 4)
                    if n >= 4:
                        pe.wait_ge(qkv_done, 6 * p + n - 3)
                        pe.wait_ge(qk_lo, 4 * p + n - 3)
                    project(pe, k, w_hi[:, j], w_lo[:, j], h_hi, h_lo, hf, bank(k, n % 4)).then_inc(projd, 1)
                pe.wait_ge(cat_done, 2 * p + 2)
                for n in range(2):
                    pe.wait_ge(qkv_done, 6 * p + 5 + n)
                    for m in range(4):
                        mm = pe.transpose(ps[:, 4 + n, m * P:(m + 1) * P],
                                          v_f[:, (4 * n + m) * P:(4 * n + m + 1) * P], ident[:])
                    mm.then_inc(vturn, 1)
                pe.wait_ge(qk_lo, 4 * p + 4)
                for u in range(U + 3):
                    if u < U:
                        i, h = units[u]
                        if u >= 2:
                            pe.wait_ge(sig_done, 2 * U * p + 2 * (u - 1))
                        for s in range(0, nk(i), HALF):
                            e = min(s + HALF, nk(i))
                            for n, (q, k_) in enumerate(((q_hi, k_hi), (q_lo, k_hi), (q_hi, k_lo))):
                                mm = pe.matmul(bank(k, 2 * (u % 2) + s // HALF, e - s), q[:, h, i * P:(i + 1) * P],
                                               k_[:, s:e], start=(n == 0), stop=(n == 2))
                        mm.then_inc(z_done, 1)
                    if 2 <= u < U + 2:
                        i, h = units[u - 2]
                        pe.wait_ge(w_done, U * p + u - 1 + 2)
                        for m in range(nturn[u - 2]):
                            n = before[u - 2] + m
                            if n >= 2:
                                pe.wait_ge(wT_done, TURNS * p + n - 1)
                            else:
                                pe.wait_ge(v_done, 2 * p + n + 1)
                            for s in range(4 * m, min(4 * m + 4, i + 1)):
                                mm = pe.transpose(ps[:, 4 + n % 2, (s - 4 * m) * P:(s - 4 * m + 1) * P],
                                                  beta[:, (u - 2) % 2, s * P:(s + 1) * P], ident[:])
                            mm.then_inc(wturn, 1)
                    if u >= 3:
                        i, h = units[u - 3]
                        pe.wait_ge(wT_done, TURNS * p + before[u - 3] + nturn[u - 3])
                        if u == 3:
                            pe.wait_ge(v_done, 2 * p + 2)
                        for s in range(i + 1):
                            mm = pe.matmul(ps[:, 6 + i // 4, (i % 4) * P:(i % 4 + 1) * P], v[:, h, s, :],
                                           wT[:, (u - 3) % 2, s * P:(s + 1) * P],
                                           start=(s == 0 and h == 0), stop=(s == i and h == 1))
                        mm.then_inc(pv_done, 1)


def linear_attention(k, c, h_hi, h_lo, cat):
    nc, sb, sem, ps, a, ident, ones, V, A, G = (
        k[n] for n in ("nc", "sb", "sem", "ps", "a", "ident", "ones", "V", "A", "G"))
    w_raw = sb("gw_raw", [P, 2, KD, P], F32, c)
    w_hi = sb("gw_hi", [P, 2, KD, P], F32R, c)
    w_lo = sb("gw_lo", [P, 2, KD, P], F32R, c)
    b_all = sb("b_all", [P, 2, T], F32, c)
    k_f = sb("k_f", [P, T], F32, c)
    qz = sb("qz", [P, 2, T], F32, c)
    vT = sb("vT", [P, 2, T], F32, c)
    v = sb("gv", [P, NT, 2 * DV], F32, c)
    r = sb("r", [P, 2, T], F32, c)
    e = sb("e", [P, 2, T], F32, c)
    ql = sb("ql", [P, 2, NT, 2, P // 2], F32, c)
    kl = sb("kl", [P, 2, T], F32, c)
    s_all = sb("s_all", [P, 2, NT, P], F32, c)
    k_dec = sb("k_dec", [P, NT, P], F32, c)
    e_last = sb("e_last", [P, NT], F32, c)
    state = sb("state", [P, 2, DV], F32, c)
    masks = sb("masks", [P, LEVELS, P // 2], F32, c)
    w2 = sb("w2", [P, KW], F32, c)
    gb = sb("gb", [P, GLA_PAIRS], F32, c)
    gn = sb("gn", [P, GLA_HEADS], F32, c)
    gn_p = sb("gn_p", [P, 2], F32, c)
    w_in_s = [sem(f"gw_in{j}") for j in range(2)]
    small = sem("g_small")
    names = "g_made g_hi g_lo g_proj g_out g_rdone g_vturn g_v g_decay g_dec_e g_dec g_kturn g_kdec g_dif g_exp " \
            "g_ql g_lev g_pred g_upd g_state g_o g_sq g_sum g_rms g_cat g_lr g_u g_x g_ln g_ql1 g_sums_read g_passed".split()
    (made, hi_done, lo_done, projd, out_done, r_done, vturn, v_done, decay, dec_e, dec, kturn, kdec_done, dif,
     exp_done, ql_done, lev_done, pred_done, upd, state_done, o_ready, sq_done, summed, rms_done, cat_done,
     lr_done, u_done, x_done, ln_done, ql1_done, sums_read, passed) = (sem(n) for n in names)
    w_dram = a["w_in"][0].rearrange("(k p) c -> p k c", p=P)
    TILES = 6
    PREDS = 4 + 2 * LEVELS
    cols = [(COL_G_Q, P), (COL_G_K, P), (COL_G_V, 2 * P), (COL_G_V + P, 2 * P), (COL_G_R, 2 * P), (COL_G_R + P, 2 * P)]

    def halves(ap, l):
        n = 1 << l
        return ap.rearrange("p (b two n) -> p b two n", two=2, n=n)

    def tile_halves(ap, l):
        return ap.rearrange("p (t b two n) -> p t b two n", t=NT, two=2, n=1 << l)

    def queries(eng, l, h):
        return eng.tensor_tensor(ql[:, l % 2, :, h, :].rearrange("p t (b n) -> p t b n", n=1 << l),
                                 tile_halves(qz[:, h], l)[:, :, :, 1, :],
                                 tile_halves(e[:, l % 2], l)[:, :, :, 1, :], ALU.mult)

    with nc.Block() as block:
        @block.sync
        def _(sp):
            sp.dma_start(w_raw[:, 1], w_dram[:, :, COL_LR:COL_LR + P]).then_inc(w_in_s[1], 16)
            sp.wait_ge(made, 1)
            sp.dma_start(w2[P - RANK:P, :], a["gla_gate_w2"][0]).then_inc(small, 16)
            with nc.allow_non_contiguous_dma(reason="biases and gains to partitions"):
                sp.dma_start(gb[:], a["gla_gate_b"][0].rearrange("(k p) -> p k", p=P)).then_inc(small, 16)
                sp.dma_start(gn[:], a["gla_norm_g"][0].rearrange("(k p) -> p k", p=P)).then_inc(small, 16)
            with sp.Fori(0, GLA_PAIRS) as p:
                for j, (c0, step) in enumerate(cols):
                    sp.wait_ge(lo_done, TILES * p + j + 1)
                    sp.dma_start(w_raw[:, j % 2], w_dram[:, :, bass.ds(p * step + c0, P)]).then_inc(w_in_s[j % 2], 16)
            for j in range(2):
                sp.wait_ge(lo_done, TILES * GLA_PAIRS + j + 1)
                with nc.allow_non_contiguous_dma(reason="a stand-in for a tile that nothing uses"):
                    sp.dma_start(w_raw[0:1, j, 0, :], w_dram[0:1, 0, 0:P]).then_inc(w_in_s[j], 16)

        @block.gpsimd
        def _(pool):
            pool.memset(w2[:], 0.0).then_inc(made, 1)
            pool.memset(kl[:], 0.0).then_inc(made, 1)
            pool.memset(qz[:], 0.0).then_inc(made, 1)
            G.step(pool.memset(masks[:], 1.0))
            for l in range(LEVELS):
                n = 1 << l
                nb = P // (2 * n)
                m = masks[:, l, :].rearrange("p (b n) -> p b n", n=n)
                lo, hi = [[-2 * n, nb]], [[2 * n, nb]]
                if nb == 1:
                    m, lo, hi = masks[:, l, :], [], []
                if n > 1:
                    lo, hi = lo + [[0, n]], hi + [[0, n]]
                else:
                    m = masks[:, l, :]
                G.step(pool.affine_select(out=m, in_=m, compare_op=ALU.is_ge, fill=0.0, base=0,
                                          pattern=lo, channel_multiplier=1))
                G.step(pool.affine_select(out=m, in_=m, compare_op=ALU.is_ge, fill=0.0, base=n - 1,
                                          pattern=hi, channel_multiplier=-1))
            pool.memset(s_all[:], 0.0).then_inc(made, 1)
            pool.memset(ql[:], 0.0).then_inc(made, 1)
            pool.wait_ge(made, 5)
            with pool.Fori(0, GLA_PAIRS) as p:
                pool.wait_ge(dec_e, 3 * p + 3)
                pool.wait_ge(v_done, 4 * p + 4)
                pool.tensor_tensor(vT[:, 1], k_f[:], e[:, 1], ALU.mult).then_inc(dec, 1)
                for l in range(LEVELS):
                    pool.wait_ge(exp_done, LEVELS * p + l + 1)
                    if l >= 2:
                        pool.wait_ge(lev_done, (LEVELS + 1) * p + l)
                    n = 1 << l
                    queries(pool, l, 0).then_inc(ql_done, 1)
                    pool.tensor_tensor(halves(kl[:, l % 2], l)[:, :, 0, :], halves(k_f[:], l)[:, :, 0, :],
                                       halves(e[:, l % 2], l)[:, :, 0, :], ALU.mult).then_inc(ql_done, 1)

        def split_hi(act, p, j):
            act.wait_ge(w_in_s[j % 2], 16 * (TILES // 2) * p + 16 * (j // 2 + 1) + 16 * (j % 2))
            if not (isinstance(p, int) and j == 0):
                act.wait_ge(projd, 2 * TILES * p + 2 * j)
            act.activation(w_hi[:, j % 2], w_raw[:, j % 2], ACT.Copy).then_inc(hi_done, 1)

        def split_lo(dve, p, j):
            dve.wait_ge(hi_done, TILES * p + j + 2)
            dve.tensor_tensor(w_lo[:, j % 2], w_raw[:, j % 2], w_hi[:, j % 2].bitcast(F32), ALU.subtract)\
               .then_inc(lo_done, 1)

        def evict_projection(act, p, j):
            for hf in range(2):
                n = 2 * j + hf
                act.wait_ge(projd, 2 * TILES * p + n + 1 + 2)
                dst = slice(hf * HALF, (hf + 1) * HALF)
                if j == 0:
                    for h in range(2):
                        rows = slice(DK * h, DK * (h + 1))
                        ins = act.activation(qz[rows, h, dst], bank(k, 4 + n % 4)[rows], ACT.Copy, scale=DK ** -0.5)
                    ins.then_inc(out_done, 1)
                elif j == 1:
                    act.activation(k_f[:, dst], bank(k, 4 + n % 4), ACT.Copy).then_inc(out_done, 1)
                elif j < 4:
                    act.activation(vT[:, j - 2, dst], bank(k, 4 + n % 4), ACT.Copy).then_inc(out_done, 1)
                else:
                    act.wait_ge(cat_done, 2 * p + 2)
                    act.activation(r[:, j - 4, dst], bank(k, 4 + n % 4), ACT.Sigmoid).then_inc(out_done, 1)

        @block.scalar
        def _(act):
            act.wait_ge(w_in_s[1], 16)
            act.activation(w_hi[:, 1], w_raw[:, 1], ACT.Copy).then_inc(hi_done, 1)
            for n in range(2):
                act.wait_ge(projd, n + 1)
                act.activation(vT[:, 0, n * HALF:(n + 1) * HALF], bank(k, n), ACT.Copy).then_inc(lr_done, 1)
            for j in range(2):
                split_hi(act, 0, j)
            act.wait_ge(made, 5)
            act.wait_ge(x_done, 4)
            A.step(act.activation(e[:], b_all[:], ACT.Abs))
            A.step(act.activation(e[:], e[:], ACT.Exp, scale=-1.0))
            act.activation(e[:], e[:], ACT.Ln, bias=1.0).then_inc(ln_done, 1)
            with act.Fori(0, GLA_PAIRS) as p:
                for j in range(TILES):
                    evict_projection(act, p, j)
                    if j + 2 < TILES:
                        split_hi(act, p, j + 2)
                    if j == 3:
                        act.wait_ge(decay, p + 1)
                        act.activation(e[:, 0], b_all[:, 0], ACT.Exp).then_inc(dec_e, 1)
                        act.activation(e_last[:], b_all[:, 0, P - 1:T:P], ACT.Exp).then_inc(dec_e, 1)
                        act.activation(e[:, 1], e[:, 1], ACT.Exp).then_inc(dec_e, 1)
                for l in range(LEVELS):
                    act.wait_ge(dif, 2 * LEVELS * p + 2 * l + 2)
                    act.activation(e[:, l % 2], e[:, l % 2], ACT.Exp).then_inc(exp_done, 1)
                act.wait_ge(o_ready, NT * p + NT)
                for h in range(2):
                    o = ps[:, 2 * h:2 * h + 2, :].rearrange("p b n -> p (b n)")
                    act.activation(e[:, h], o, ACT.Square).then_inc(sq_done, 1)
                for j in range(2):
                    split_hi(act, p + 1, j)
                for h in range(2):
                    act.wait_ge(summed, 2 * p + h + 1)
                    s = ps[:, 4 + 2 * h:6 + 2 * h, :].rearrange("p b n -> p (b n)")
                    act.activation(kl[:, h], s, ACT.Ln, bias=k["eps_t"][:], scale=1.0 / DV).then_inc(ln_done, 1)
                for h in range(2):
                    act.wait_ge(ln_done, 2 * p + h + 2)
                    act.activation(kl[:, h], kl[:, h], ACT.Exp, scale=-0.5).then_inc(rms_done, 1)
                    act.sem_inc(sums_read, 1)

        @block.vector
        def _(dve):
            dve.sem_inc(lo_done, 1)
            dve.sem_inc(cat_done, 2)
            dve.wait_ge(hi_done, 1)
            dve.tensor_tensor(w_lo[:, 1], w_raw[:, 1], w_hi[:, 1].bitcast(F32), ALU.subtract).then_inc(lo_done, 1)
            for j in range(2):
                split_lo(dve, 0, j)
            dve.wait_ge(made, 5)
            for n in range(4):
                pr, hf = divmod(n, 2)
                dve.wait_ge(u_done, n + 1)
                dve.wait_ge(small, 48)
                dve.tensor_scalar(b_all[:, pr, hf * HALF:(hf + 1) * HALF], bank(k, n), gb[:, pr:pr + 1], None,
                                  ALU.add).then_inc(x_done, 1)
            dve.wait_ge(x_done, 4)
            dve.wait_ge(ln_done, 1)
            V.step(dve.tensor_scalar(b_all[:], b_all[:], 0.0, None, ALU.min))
            V.step(dve.tensor_tensor(b_all[:], b_all[:], e[:], ALU.subtract))
            V.step(dve.tensor_scalar(b_all[:], b_all[:], 1.0 / TAU, None, ALU.mult))
            for pr in range(2):
                for t in range(NT):
                    x = b_all[:, pr, t * P:(t + 1) * P]
                    V.mark(dve.tensor_tensor_scan(e[:, pr, t * P:(t + 1) * P], x, x, 0.0, ALU.add, ALU.bypass))
            V.join()
            V.step(dve.tensor_copy(b_all[:], e[:]))
            PER = 4

            def exponents(l):
                bl, el = halves(b_all[:, 0], l), halves(e[:, l % 2], l)
                n, nb = 1 << l, T >> (l + 1)
                ref = bl[:, :, 0, n - 1:n].to_broadcast([P, nb, n])
                dve.tensor_tensor(el[:, :, 0, :], ref, bl[:, :, 0, :], ALU.subtract).then_inc(dif, 1)
                dve.tensor_tensor(el[:, :, 1, :], bl[:, :, 1, :], ref, ALU.subtract).then_inc(dif, 1)

            with dve.Fori(0, GLA_PAIRS) as p:
                base = V.enter(p, PER)
                dve.wait_ge(cat_done, 2 * p + 2)
                V.step(dve.tensor_copy(gn_p[:], gn[:, bass.ds(2 * p, 2)]))
                bt = b_all[:, 0].rearrange("p (t n) -> p t n", n=P)
                dve.tensor_tensor(e[:, 1].rearrange("p (t n) -> p t n", n=P), bt[:, :, P - 1:P].to_broadcast([P, NT, P]),
                                  bt, ALU.subtract).then_inc(decay, 1)
                for j in range(2, TILES):
                    split_lo(dve, p, j)
                for j in range(2):
                    for hf in range(2):
                        dst = slice(hf * HALF, (hf + 1) * HALF)
                        n = 8 + 2 * j + hf
                        dve.wait_ge(out_done, 2 * TILES * p + n + 1)
                        dve.tensor_tensor(r[:, j, dst], bank(k, 4 + n % 4), r[:, j, dst], ALU.mult).then_inc(r_done, 1)
                for n in range(4):
                    dve.wait_ge(vturn, 4 * p + n + 1)
                    dve.tensor_copy(v[:, 2 * n:2 * n + 2, :].rearrange("p t n -> p (t n)"), bank(k, n)).then_inc(v_done, 1)
                dve.wait_ge(dec_e, 3 * p + 3)
                for h in range(2):
                    rows = slice(DK * h, DK * (h + 1))
                    dve.tensor_tensor(vT[rows, 0], qz[rows, h], e[rows, 0], ALU.mult).then_inc(dec, 1)
                dve.wait_ge(dec, 3 * p + 3)
                for l in range(2):
                    exponents(l)
                for n in range(2):
                    dve.wait_ge(kturn, 2 * p + n + 1)
                    dve.tensor_copy(k_dec[:, 4 * n:4 * n + 4, :].rearrange("p t n -> p (t n)"), bank(k, 4 + n))\
                       .then_inc(kdec_done, 1)
                dve.wait_ge(lev_done, (LEVELS + 1) * p + 1)
                dve.sem_inc(passed, 1)
                eye = ident[:].bitcast(I32).unsqueeze(1).unsqueeze(1).to_broadcast([P, 2, 2, P])
                for m in range(4):
                    dst = s_all[:, :, 2 * m:2 * m + 2, :].rearrange("p h q n -> p q h n")
                    src = bank(k, m).rearrange("p (q h n) -> p q h n", q=2, n=P)
                    dve.copy_predicated(dst, eye, src).then_inc(pred_done, 1)
                for l in range(LEVELS + 2):
                    if 2 <= l < LEVELS:
                        dve.wait_ge(ql_done, 2 * LEVELS * p + 2 * (l - 2) + 2)
                        dve.wait_ge(ql1_done, LEVELS * p + (l - 2) + 1)
                        exponents(l)
                    if 1 <= l <= LEVELS:
                        m = l - 1
                        dve.wait_ge(exp_done, LEVELS * p + m + 1)
                        if m >= 2:
                            dve.wait_ge(lev_done, (LEVELS + 1) * p + m)
                        queries(dve, m, 1).then_inc(ql1_done, 1)
                    if l >= 2:
                        m = l - 2
                        n, nb = 1 << m, P >> (m + 1)
                        dve.wait_ge(lev_done, (LEVELS + 1) * p + m + 2)
                        for h in range(2):
                            dst = halves(s_all[:, h].rearrange("p t n -> p (t n)"), m)[:, :, 1, :]
                            dst = dst.rearrange("p (q b) n -> p q b n", q=NT)
                            msk = masks[:, m, :].bitcast(I32).rearrange("p (b n) -> p b n", n=n).unsqueeze(1)\
                                .to_broadcast([P, NT, nb, n])
                            two_banks = ps[:, 4 + 2 * (m % 2):6 + 2 * (m % 2), :].rearrange("p c n -> p (c n)")
                            src = two_banks.rearrange("p (q h b n) -> p h q b n", h=2, q=NT, n=n)[:, h]
                            dve.wait_ge(pred_done, PREDS * p + 4 + 2 * m)
                            dve.sem_inc(passed, 1)
                            dve.copy_predicated(dst, msk, src).then_inc(pred_done, 1)
                for t in range(NT):
                    dve.wait_ge(upd, NT * p + t + 1)
                    for h in range(2):
                        rows = slice(DK * h, DK * (h + 1))
                        new = bank(k, 4 + t % 2)[rows, h * DV:(h + 1) * DV]
                        if t == 0:
                            ins = dve.tensor_copy(state[rows, 1, :], new)
                        else:
                            if h == 0:
                                dve.wait_ge(state_done, 2 * NT * p + 2 * t)
                                if t >= 2:
                                    dve.wait_ge(o_ready, NT * p + t)
                            ins = dve.scalar_tensor_tensor(state[rows, (t + 1) % 2, :], state[rows, t % 2, :],
                                                           e_last[rows, t:t + 1], new, ALU.mult, ALU.add)
                        ins.then_inc(state_done, 1)
                for j in range(2):
                    split_lo(dve, p + 1, j)
                for h in range(2):
                    dve.wait_ge(rms_done, 2 * p + h + 1)
                    o = ps[:, 2 * h:2 * h + 2, :].rearrange("p b n -> p (b n)")
                    V.step(dve.tensor_tensor(e[:, h], o, kl[:, h], ALU.mult))
                    dve.scalar_tensor_tensor(cat[:, bass.ds(2 * p + (SB_PAIRS + h), 1), :].rearrange("p o n -> p (o n)"),
                                             e[:, h], gn_p[:, h:h + 1], r[:, h], ALU.mult, ALU.mult).then_inc(cat_done, 1)
                V.step(dve.tensor_copy(b_all[:, 0], b_all[:, 1]))
                V.leave(base, PER, GLA_PAIRS)

        @block.tensor
        def _(pe):
            for hf in range(2):
                pe.wait_ge(lo_done, 2)
                project(pe, k, w_hi[:, 1], w_lo[:, 1], h_hi, h_lo, hf, bank(k, hf)).then_inc(projd, 1)
            pe.sem_inc(sums_read, 2)
            pe.wait_ge(small, 48)
            pe.wait_ge(lr_done, 2)
            for n in range(4):
                pr, hf = divmod(n, 2)
                pe.matmul(bank(k, n), w2[:, pr * P:(pr + 1) * P], vT[:, 0, hf * HALF:(hf + 1) * HALF],
                          start=True, stop=True).then_inc(u_done, 1)
            with pe.Fori(0, GLA_PAIRS) as p:
                pe.wait_ge(sums_read, 2 * p + 2)
                for n in range(2 * TILES):
                    j, hf = divmod(n, 2)
                    if hf == 0:
                        pe.wait_ge(lo_done, TILES * p + j + 3)
                    if n >= 4:
                        pe.wait_ge(out_done, 2 * TILES * p + n - 3)
                    project(pe, k, w_hi[:, j % 2], w_lo[:, j % 2], h_hi, h_lo, hf, bank(k, 4 + n % 4)).then_inc(projd, 1)
                pe.wait_ge(out_done, 2 * TILES * p + 8)
                pe.wait_ge(x_done, 4)
                pe.wait_ge(cat_done, 2 * p + 2)
                for n in range(4):
                    for m in range(4):
                        t, h = 2 * n + m // 2, m % 2
                        mm = pe.transpose(ps[:, n, m * P:(m + 1) * P], vT[:, h, t * P:(t + 1) * P], ident[:])
                    mm.then_inc(vturn, 1)
                pe.wait_ge(v_done, 4 * p + 4)
                for t in range(NT):
                    mm = pe.matmul(ps[:, t // 2, (t % 2) * 2 * P:(t % 2 + 1) * 2 * P], k_f[:, t * P:(t + 1) * P],
                                   qz[:, :, t * P:(t + 1) * P], start=True, stop=True)
                mm.then_inc(lev_done, 1)
                pe.wait_ge(dec, 3 * p + 3)
                pe.wait_ge(r_done, 4 * p + 4)
                for n in range(2):
                    pe.wait_ge(v_done, 4 * p + n + 1)
                    for m in range(4):
                        mm = pe.transpose(ps[:, 4 + n, m * P:(m + 1) * P], vT[:, 1, (4 * n + m) * P:(4 * n + m + 1) * P],
                                          ident[:])
                    mm.then_inc(kturn, 1)
                pe.wait_ge(kdec_done, 2 * p + 2)
                pe.wait_ge(v_done, 4 * p + 4)
                for l in range(LEVELS):
                    pe.wait_ge(ql_done, 2 * LEVELS * p + 2 * l + 2)
                    pe.wait_ge(ql1_done, LEVELS * p + l + 1)
                    if l >= 2:
                        pe.wait_ge(pred_done, PREDS * p + 2 * l + 2)
                    for t in range(NT):
                        mm = pe.matmul(ps[:, 4 + 2 * (l % 2) + t // 4, (t % 4) * P:(t % 4 + 1) * P],
                                       kl[:, l % 2, t * P:(t + 1) * P],
                                       ql[:, l % 2, t, :, :].rearrange("p h n -> p (h n)"), start=True, stop=True)
                    mm.then_inc(lev_done, 1)
                pe.wait_ge(pred_done, PREDS * p + PREDS)
                for t in range(NT):
                    if t >= 2:
                        pe.wait_ge(state_done, 2 * NT * p + 2 * (t - 1))
                    if t < NT:
                        pe.matmul(bank(k, 4 + t % 2, 2 * DV), k_dec[:, t, :], v[:, t, :], start=True, stop=True).then_inc(upd, 1)
                    if t >= 1:
                        pe.wait_ge(state_done, 2 * NT * p + 2 * t)
                    for h in range(2):
                        rows = slice(DK * h, DK * (h + 1))
                        out = ps[:, 2 * h + t // 4, (t % 4) * P:(t % 4 + 1) * P]
                        mm = pe.matmul(out, v[:, t, h * DV:(h + 1) * DV], s_all[:, h, t, :], start=True, stop=(t == 0))
                        if t >= 1:
                            mm = pe.matmul(out, state[rows, t % 2, :], vT[rows, 0, t * P:(t + 1) * P],
                                           start=False, stop=True)
                    mm.then_inc(o_ready, 1)
                pe.wait_ge(state_done, 2 * NT * p + 2 * NT)
                for h in range(2):
                    pe.wait_ge(sq_done, 2 * p + h + 1)
                    for hf in range(2):
                        mm = pe.matmul(bank(k, 4 + 2 * h + hf), ones[:], e[:, h, hf * HALF:(hf + 1) * HALF],
                                       start=True, stop=True)
                    mm.then_inc(summed, 1)


def mix_out(k, c, cat, logits):
    nc, sb, sem, ps, a, ident = (k[n] for n in ("nc", "sb", "sem", "ps", "a", "ident"))
    wo_raw = sb("wo_raw", [P, KD, D], F32, c)
    wo_hi = sb("wo_hi", [P, KD, D], F32R, c)
    wo_lo = sb("wo_lo", [P, KD, D], F32R, c)
    cat_hi = sb("cat_hi", [P, 2, KD, P], F32R, c)
    cat_lo = sb("cat_lo", [P, 2, KD, P], F32R, c)
    x = sb("x_res", [P, 2, D], F32, c)
    x1 = sb("x1", [P, 2, D], F32, c)
    sq = sb("sq", [P, D], F32, c)
    h2 = sb("h2", [P, 2, D], F32, c)
    g2 = sb("g2", [P, D], F32, c)
    h2T = sb("h2T", [P, KD, P], F32, c)
    wr = sb("wr", [P, KD, LOGITS], F32, c)
    rb = sb("rb", [P, LOGITS], F32, c)
    ss, rms, inv = (sb(n, [P, 2], F32, c) for n in ("o_ss", "o_rms", "o_inv"))
    wo_in = [sem(f"wo_in{kd}") for kd in range(KD // 2)]
    x_in = [sem(f"xr_in{j}") for j in range(2)]
    x1_out = [sem(f"x1_out{j}") for j in range(2)]
    h2_out = [sem(f"h2_out{j}") for j in range(2)]
    small = sem("o_small")
    names = "o_wohi o_wolo o_cathi o_catlo o_mm o_x1 o_ss o_rms o_inv o_h2 o_turn o_h2T o_lg o_logits".split()
    (wohi, wolo, cathi, catlo, mm_done, x1_done, ss_done, rms_done, inv_done, h2_done, turned, h2T_done, lg,
     logit_done) = (sem(n) for n in names)
    with nc.Block() as block:
        @block.sync
        def _(sp):
            for kd in range(KD):
                sp.dma_start(wo_raw[:, kd], a["w_out"][0, kd * P:(kd + 1) * P, :]).then_inc(wo_in[kd // 2], 16)
            sp.dma_start(g2[:], a["ln2_g"][0:1].partition_broadcast(P).rearrange("p o n -> p (o n)")).then_inc(small, 16)
            sp.dma_start(wr[:, :, 0:GROUPS], a["w_group"][0].rearrange("(k p) n -> p k n", p=P)).then_inc(small, 16)
            sp.dma_start(wr[:, :, GROUPS:LOGITS], a["w_expert"][0].rearrange("(k p) n -> p k n", p=P)).then_inc(small, 16)
            sp.dma_start(rb[:, 0:GROUPS], a["b_group"][0:1].partition_broadcast(P).rearrange("p o n -> p (o n)")).then_inc(small, 16)
            sp.dma_start(rb[:, GROUPS:LOGITS], a["b_expert"][0:1].partition_broadcast(P).rearrange("p o n -> p (o n)")).then_inc(small, 16)
            for t in range(NT + 2):
                if t >= 2:
                    sp.wait_ge(x1_done, t - 1)
                    sp.dma_start(k["x1_dram"][(t - 2) * P:(t - 1) * P, :], x1[:, t % 2]).then_inc(x1_out[t % 2], 16)
                if t < NT:
                    sp.dma_start(x[:, t % 2], a["x"][0, t * P:(t + 1) * P, :]).then_inc(x_in[t % 2], 16)
                if t >= 2:
                    sp.wait_ge(h2_done, t - 1)
                    sp.dma_start(k["h2_dram"][(t - 2) * P:(t - 1) * P, :], h2[:, t % 2]).then_inc(h2_out[t % 2], 16)
            for j in range(2):
                sp.wait_ge(x1_out[j], 16 * NT // 2)
                sp.wait_ge(h2_out[j], 16 * NT // 2)

        @block.scalar
        def _(act):
            for t in range(-1, NT):
                if t == 0:
                    for kd in range(KD):
                        act.wait_ge(wo_in[kd // 2], 32)
                        act.activation(wo_hi[:, kd], wo_raw[:, kd], ACT.Copy).then_inc(wohi, 1)
                if t + 1 < NT:
                    if t >= 1:
                        act.wait_ge(mm_done, t)
                    act.activation(cat_hi[:, (t + 1) % 2], cat[:, :, (t + 1) * P:(t + 2) * P], ACT.Copy).then_inc(cathi, 1)
                if t >= 0:
                    j = t % 2
                    act.wait_ge(x1_done, t + 1)
                    if t >= 1:
                        act.wait_ge(ss_done, t)
                    act.activation(sq[:], x1[:, j], ACT.Square, accum_out=ss[:, j:j + 1]).then_inc(ss_done, 1)
                    act.wait_ge(ss_done, t + 1)
                    act.activation(rms[:, j:j + 1], ss[:, j:j + 1], ACT.Sqrt, bias=k["eps_t"][:],
                                   scale=1.0 / D).then_inc(rms_done, 1)

        @block.vector
        def _(dve):

            for t in range(-1, NT + 2):
                j = t % 2
                if t == 0:
                    for kd in range(KD):
                        dve.wait_ge(wohi, kd + 1)
                        dve.tensor_tensor(wo_lo[:, kd], wo_raw[:, kd], wo_hi[:, kd].bitcast(F32),
                                          ALU.subtract).then_inc(wolo, 1)
                    dve.wait_ge(small, 80)
                if t + 1 < NT:
                    dve.wait_ge(cathi, t + 2)
                    dve.tensor_tensor(cat_lo[:, 1 - j], cat[:, :, (t + 1) * P:(t + 2) * P], cat_hi[:, 1 - j].bitcast(F32),
                                      ALU.subtract).then_inc(catlo, 1)
                if 0 <= t < NT:
                    dve.wait_ge(x_in[j], 16 * (t // 2) + 16)
                    dve.wait_ge(mm_done, t + 1)
                    if t >= 2:
                        dve.wait_ge(x1_out[j], 16 * (t // 2))
                    dve.tensor_tensor(x1[:, j], ps[:, 2 * j:2 * j + 2, :].rearrange("p b n -> p (b n)"), x[:, j],
                                      ALU.add).then_inc(x1_done, 1)
                if 1 <= t <= NT:
                    if t >= 2:
                        dve.wait_ge(lg, t - 1)
                    for m in range(2):
                        dve.wait_ge(turned, 2 * (t - 1) + m + 1)
                        dve.tensor_copy(h2T[:, 4 * m:4 * m + 4, :].rearrange("p k n -> p (k n)"), bank(k, 4 + m))\
                           .then_inc(h2T_done, 1)
                if 0 <= t < NT:
                    dve.wait_ge(rms_done, t + 1)
                    dve.reciprocal(inv[:, j:j + 1], rms[:, j:j + 1]).then_inc(inv_done, 1)
                    dve.wait_ge(inv_done, t + 1)
                    if t >= 2:
                        dve.wait_ge(h2_out[j], 16 * (t // 2))
                    dve.scalar_tensor_tensor(h2[:, j], x1[:, j], inv[:, j:j + 1], g2[:], ALU.mult, ALU.mult).then_inc(h2_done, 1)
                if t >= 2:
                    dve.wait_ge(lg, t - 1)
                    dve.tensor_tensor(logits[:, t - 2, :], bank(k, 6, LOGITS), rb[:], ALU.add).then_inc(logit_done, 1)

        @block.tensor
        def _(pe):
            for t in range(NT + 2):
                j = t % 2
                if t < NT:
                    pe.wait_ge(catlo, t + 1)
                    if t >= 2:
                        pe.wait_ge(x1_done, t - 1)
                    for hf in range(2):
                        n = 0
                        cols = slice(hf * HALF, (hf + 1) * HALF)
                        for kd in range(KD):
                            if hf == 0 and t == 0:
                                pe.wait_ge(wolo, kd + 1)
                            for x_, w_ in ((cat_hi, wo_hi), (cat_lo, wo_hi), (cat_hi, wo_lo)):
                                mm = pe.matmul(bank(k, 2 * j + hf), x_[:, j, kd, :], w_[:, kd, cols], start=(n == 0),
                                               stop=(n == 3 * KD - 1))
                                n += 1
                    mm.then_inc(mm_done, 1)
                if t >= 2:
                    pe.wait_ge(h2T_done, 2 * (t - 1))
                    if t >= 3:
                        pe.wait_ge(logit_done, t - 2)
                    for kd in range(KD):
                        mm = pe.matmul(bank(k, 6, LOGITS), h2T[:, kd, :], wr[:, kd, :], start=(kd == 0), stop=(kd == KD - 1))
                    mm.then_inc(lg, 1)
                if 1 <= t <= NT:
                    pe.wait_ge(h2_done, t)
                    if t >= 2:
                        pe.wait_ge(h2T_done, 2 * (t - 1))
                    for m in range(2):
                        for q in range(4):
                            mm = pe.transpose(ps[:, 4 + m, q * P:(q + 1) * P],
                                              h2[:, 1 - j, (4 * m + q) * P:(4 * m + q + 1) * P], ident[:])
                        mm.then_inc(turned, 1)


def expert_weights(k, c):
    sb, sem, a = k["sb"], k["sem"], k["a"]
    shapes = dict(g=[P, KD, FF], u=[P, KD, FF], d=[P, KF, D])
    w = {n: (sb(f"w_{n}", shape, F32, c), a[f"exp_w_{name}"][0], sem(f"e_{n}_in"))
         for (n, shape), name in zip(shapes.items(), ("gate", "up", "down"))}
    halves = {n: (sb(f"{n}_hi", shape, F32R, c), sb(f"{n}_lo", shape, F32R, c), sem(f"e_{n}hi"), sem(f"e_{n}lo"))
              for n, shape in shapes.items()}
    return w, halves


def route(k, c, logits, experts_w):
    nc, sb, sem, ps, ident, ones, V = (k[n] for n in ("nc", "sb", "sem", "ps", "ident", "ones", "V"))
    MB = MAX_BLOCKS + 4
    pos = sb("pos", [P, NT, EXPERTS], F32, c)
    pay = sb("pay", [P, NT, EXPERTS, 4], F32, c)
    block_e = sb("block_e", [P, MB], I32, c)
    block_j = sb("block_j", [P, MB], F32, c)
    halves = sb("halves", [P, 2], I32, c)
    tables = (pos, pay, block_e, block_j, halves)
    tmp = ExitStack()
    c = tmp
    weights, parts = experts_w
    pieces = [("g", slice(0, KD // 2)), ("g", slice(KD // 2, KD)), ("u", slice(0, KD))]
    JX = -(-T // CAP) - 1
    iota4 = sb("iota4", [P, GROUPS], F32, c)
    iota8 = sb("iota8", [P, PER_GROUP], F32, c)
    tok = sb("tok", [P, NT], F32, c)
    iota_e = sb("iota_e", [P, EXPERTS, JX], F32, c)
    iota_j = sb("iota_j", [P, EXPERTS, JX], F32, c)
    odd = sb("odd", [P, MAX_HALVES - EXPERTS // 2], F32, c)
    part1 = sb("part1", [P, 1], F32, c)
    before = sb("before", [P, P], F32, c)
    S4 = [P, NT, GROUPS]
    S8 = [P, NT, PER_GROUP]
    S32 = [P, NT, GROUPS, PER_GROUP]
    t4, t4b, og, e4 = (sb(n, S4, F32, c) for n in ("t4", "t4b", "og", "e4"))
    t32v = sb("t32v", [P, NT, PER_GROUP, GROUPS], F32, c)
    sel, t8, o1, o2, pr = (sb(n, S8, F32, c) for n in ("sel", "t8", "o1", "o2", "pr"))
    t32, m1, m2, am = (sb(n, S32, F32, c) for n in ("t32", "m1", "m2", "am"))
    gmax, gsum, cmax, smax, ssum, p1, p2, den, w1, w2_ = (
        sb(n, [P, NT], F32, c) for n in ("gmax", "gsum", "cmax", "smax", "ssum", "p1", "p2", "den", "gw1", "gw2"))
    tot = sb("tot", [P, NT, EXPERTS], F32, c)
    off = sb("off", [P, NT + 1, EXPERTS], F32, c)
    fl, rank, t320 = (sb(n, [P, EXPERTS, JX], F32, c) for n in ("fl", "rank", "t320"))
    ejv = sb("ejv", [P, 4], F32, c)
    diag = sb("diag", [P, 2, P], F32, c)
    made, need_exp, expd, placed, place_mm, ext, ext_mm = (
        sem(n) for n in ("r_made", "r_need", "r_exp", "r_place", "r_placemm", "r_ext", "r_extmm"))

    def over(ap, shape):
        return ap.unsqueeze(len(ap.shape)).to_broadcast(shape)

    with nc.Block() as block:
        @block.sync
        def _(sp):
            for w, w_dram, w_in in weights.values():
                sp.dma_start(w[:], w_dram[0].rearrange("(k p) n -> p k n", p=P)).then_inc(w_in, 16)
            for n, count in (("g", 2), ("u", 1)):
                w, w_dram, w_in = weights[n]
                sp.wait_ge(parts[n][3], count)
                sp.dma_start(w[:], w_dram[1].rearrange("(k p) n -> p k n", p=P)).then_inc(w_in, 16)

        @block.gpsimd
        def _(pool):
            iota = dict(allow_small_or_imprecise_dtypes=True)
            pool.iota(iota4[:], [[-1, GROUPS]], base=GROUPS, channel_multiplier=0, **iota).then_inc(made, 1)
            pool.iota(iota8[:], [[-1, PER_GROUP]], base=PER_GROUP, channel_multiplier=0, **iota).then_inc(made, 1)
            pool.iota(tok[:], [[P, NT]], base=0, channel_multiplier=1, **iota).then_inc(made, 1)
            pool.iota(iota_e[:], [[1, EXPERTS], [0, JX]], base=0, channel_multiplier=0, **iota).then_inc(made, 1)
            pool.iota(iota_j[:], [[0, EXPERTS], [1, JX]], base=1, channel_multiplier=0, **iota).then_inc(made, 1)
            pool.iota(part1[:], [[0, 1]], base=1, channel_multiplier=1, **iota).then_inc(made, 1)
            pool.iota(odd[:], [[2, MAX_HALVES - EXPERTS // 2]], base=1, channel_multiplier=0, **iota).then_inc(made, 1)
            pool.memset(pay[:, :, :, 2:3], 1.0).then_inc(made, 1)
            pool.affine_select(out=before[:], in_=ones[:], compare_op=ALU.is_gt, fill=0.0, base=0,
                               pattern=[[1, P]], channel_multiplier=-1).then_inc(made, 1)
            for n, part in pieces:
                (w, _, w_in), (hi, lo, hi_done, lo_done) = weights[n], parts[n]
                pool.wait_ge(hi_done, 2 if part.start else 1)
                pool.tensor_tensor(lo[:, part], w[:, part], hi[:, part].bitcast(F32), ALU.subtract).then_inc(lo_done, 1)

        @block.scalar
        def _(act):
            act.wait_ge(need_exp, 1)
            act.activation(e4[:], t4[:], ACT.Exp).then_inc(expd, 1)
            act.wait_ge(need_exp, 2)
            act.activation(pr[:], t8[:], ACT.Exp).then_inc(expd, 1)
            for n, part in pieces:
                (w, _, w_in), (hi, _, hi_done, _) = weights[n], parts[n]
                act.wait_ge(w_in, 16)
                act.activation(hi[:, part], w[:, part], ACT.Copy).then_inc(hi_done, 1)

        @block.vector
        def _(dve):
            tt, ts, red = dve.tensor_tensor, dve.tensor_scalar, dve.tensor_reduce
            dve.wait_ge(made, 9)
            gl = logits[:, :, 0:GROUPS]
            el = logits[:, :, GROUPS:LOGITS].rearrange("p t (g j) -> p t j g", g=GROUPS)

            def first_of(hot, vals, top, iota_, shape, tmp_):
                V.step(tt(hot, vals, over(top, shape), ALU.is_ge))
                V.step(tt(tmp_, hot, iota_.unsqueeze(1).to_broadcast(shape), ALU.mult))
                V.step(red(cmax[:], tmp_, X, ALU.max))
                V.step(tt(hot, tmp_, over(cmax[:], shape), ALU.is_equal))

            V.step(red(gmax[:], gl, X, ALU.max))
            V.step(tt(t4[:], gl, over(gmax[:], S4), ALU.subtract))
            dve.sem_inc(need_exp, 1)
            first_of(og[:], gl, gmax[:], iota4[:], S4, t4b[:])
            dve.wait_ge(expd, 1)
            V.step(red(gsum[:], e4[:], X, ALU.add))
            V.step(tt(t32v[:], el, og[:].unsqueeze(2).to_broadcast([P, NT, PER_GROUP, GROUPS]), ALU.mult))
            V.step(red(sel[:], t32v[:], X, ALU.add))
            V.step(red(smax[:], sel[:], X, ALU.max))
            V.step(tt(t8[:], sel[:], over(smax[:], S8), ALU.subtract))
            dve.sem_inc(need_exp, 1)
            dve.wait_ge(expd, 2)
            V.step(red(ssum[:], pr[:], X, ALU.add))
            V.step(dve.reciprocal(ssum[:], ssum[:]))
            V.step(tt(pr[:], pr[:], over(ssum[:], S8), ALU.mult))
            V.step(red(p1[:], pr[:], X, ALU.max))
            first_of(o1[:], pr[:], p1[:], iota8[:], S8, t8[:])
            V.step(dve.scalar_tensor_tensor(sel[:], o1[:], -2.0, pr[:], ALU.mult, ALU.add))
            V.step(red(p2[:], sel[:], X, ALU.max))
            first_of(o2[:], sel[:], p2[:], iota8[:], S8, t8[:])
            V.step(tt(den[:], p1[:], p2[:], ALU.add))
            V.step(tt(den[:], den[:], gsum[:], ALU.mult))
            V.step(dve.reciprocal(den[:], den[:]))
            V.step(tt(w1[:], p1[:], den[:], ALU.mult))
            V.step(tt(w2_[:], p2[:], den[:], ALU.mult))
            ogb = over(og[:], S32)
            V.step(tt(m1[:], ogb, o1[:].unsqueeze(2).to_broadcast(S32), ALU.mult))
            V.step(tt(m2[:], ogb, o2[:].unsqueeze(2).to_broadcast(S32), ALU.mult))
            dve.tensor_tensor(am[:], m1[:], m2[:], ALU.add).then_inc(placed, 1)
            m1f, m2f, amf, t32f = (x[:].rearrange("p t g j -> p t (g j)") for x in (m1, m2, am, t32))
            S = [P, NT, EXPERTS]
            V.step(tt(m1f, m1f, over(w1[:], S), ALU.mult))
            V.step(tt(t32f, m2f, over(w2_[:], S), ALU.mult))
            V.step(tt(pay[:, :, :, 3], m1f, t32f, ALU.add))
            V.step(ts(m2f, m2f, float(T), None, ALU.mult))
            V.step(tt(pay[:, :, :, 1], m2f, over(tok[:], S), ALU.add))
            V.step(dve.tensor_copy(pay[:, :, :, 0], over(tok[:], S)))
            dve.wait_ge(placed, 1)
            dve.wait_ge(place_mm, 1)
            within = bank(k, 0, NT * EXPERTS).rearrange("p (t e) -> p t e", e=EXPERTS)
            V.step(dve.tensor_copy(tot[:].rearrange("p t e -> p (t e)"), bank(k, 1, NT * EXPERTS)))
            V.step(dve.memset(off[:, 0, :], 0.0))
            for t in range(NT):
                V.step(tt(off[:, t + 1, :], off[:, t, :], tot[:, t, :], ALU.add))
            V.step(tt(pos[:], within, off[:, 0:NT, :], ALU.add))
            V.step(ts(pos[:], pos[:], 1.0, None, ALU.add))
            V.step(tt(pos[:], pos[:], amf, ALU.mult))
            V.step(ts(pos[:], pos[:], -1.0, None, ALU.add))
            V.step(ts(fl[:], iota_j[:], float(CAP), None, ALU.mult))
            V.step(tt(fl[:], over(off[:, NT, :], [P, EXPERTS, JX]), fl[:], ALU.is_gt))
            flat = fl[:].rearrange("p e j -> p (e j)")
            V.step(dve.tensor_tensor_scan(rank[:].rearrange("p e j -> p (e j)"), flat, flat, 0.0, ALU.add, ALU.bypass))
            V.step(dve.tensor_copy(cmax[:, 0:1], rank[:, EXPERTS - 1, JX - 1:JX]))
            V.step(tt(rank[:], rank[:], fl[:], ALU.mult))
            V.step(ts(fl[:], rank[:], part1[:, 0:1], None, ALU.is_equal))
            for n, what in enumerate((iota_e, iota_j)):
                V.step(tt(t320[:], fl[:], what[:], ALU.mult))
                V.step(red(ejv[:, n:n + 1], t320[:].rearrange("p e j -> p (e j)"), X, ALU.add))
            V.step(red(ejv[:, 2:3], flat, X, ALU.add))
            V.step(ts(ejv[:, 2:3], ejv[:, 2:3], -2.0 * JX, 2.0 * JX, ALU.mult, ALU.add))
            V.step(tt(ejv[:, 1:2], ejv[:, 1:2], ejv[:, 2:3], ALU.add))
            V.step(ts(ejv[:, 1:2], ejv[:, 1:2], -float(CAP), None, ALU.mult))
            V.step(ts(diag[:, 0, :], ident[:], ejv[:, 0:1], None, ALU.mult))
            dve.tensor_scalar(diag[:, 1, :], ident[:], ejv[:, 1:2], None, ALU.mult).then_inc(ext, 1)
            V.step(dve.tensor_copy(block_e[:, 0:EXPERTS], iota_e[:, :, 0]))
            V.step(dve.memset(block_j[:, 0:EXPERTS], 0.0))
            dve.wait_ge(ext_mm, 1)
            V.step(dve.tensor_copy(block_e[:, EXPERTS:MB], ps[:, 2, 0:MB - EXPERTS]))
            V.step(dve.tensor_copy(block_j[:, EXPERTS:MB], ps[:, 2, P:P + MB - EXPERTS]))
            V.step(ts(odd[:], odd[:], cmax[:, 0:1], None, ALU.is_le))
            V.step(red(cmax[:, 1:2], odd[:], X, ALU.add))
            V.step(ts(halves[:, 0:1], cmax[:, 1:2], float(EXPERTS // 2), None, ALU.add))
            V.step(ts(halves[:, 1:2], cmax[:, 1:2], 2.0, float(EXPERTS), ALU.mult, ALU.add))

        @block.tensor
        def _(pe):
            pe.wait_ge(made, 9)
            pe.wait_ge(placed, 1)
            am_ = am[:].rearrange("p t g j -> p (t g j)")
            pe.matmul(bank(k, 0, NT * EXPERTS), before[:], am_, start=True, stop=True)
            pe.matmul(bank(k, 1, NT * EXPERTS), ones[:], am_, start=True, stop=True).then_inc(place_mm, 1)
            pe.wait_ge(ext, 1)
            pe.matmul(ps[:, 2, 0:2 * P], ones[:], diag[:].rearrange("p a n -> p (a n)"), start=True, stop=True).then_inc(ext_mm, 1)
    tmp.close()
    return tables


def experts(k, c, tables, w):
    nc, sb, sem, ps, ident, G = (k[n] for n in ("nc", "sb", "sem", "ps", "ident", "G"))
    pos, pay, block_e, block_j, halves = tables
    weights, parts = w
    (w_g, wg, g_in), (w_u, wu, u_in), (w_d, wd, d_in) = weights["g"], weights["u"], weights["d"]
    (g_hi, g_lo, ghi, glo), (u_hi, u_lo, uhi, ulo), (d_hi, d_lo, dhi, dlo) = parts["g"], parts["u"], parts["d"]
    place = sb("place", [P, CAP], F32, c)
    pos_b = sb("pos_b", [P, NT], F32, c)
    pay_b = sb("pay_b", [P, NT, 4], F32, c)
    hot = sb("hot", [P, NT, CAP], F32, c)
    found = sb("found", [P, 2, 4], F32, c)
    src = sb("src", [P, 1], U32, c)
    far = sb("far", [P, 1], F32, c)
    gate = sb("gate", [P, 2, 1], F32, c)
    late_far = sb("late_far", [P, 1], F32, c)
    dst = [sb(f"dst{j}", [P, 1], U32, c) for j in range(2)]
    x_g = [sb(f"x_g{j}", [P, D], F32, c) for j in range(2)]
    x_hi, x_lo = (sb(n, [P, KD, P], F32R, c) for n in ("x_hi", "x_lo"))
    hid = sb("hid", [P, FF], F32, c)
    hid_hi, hid_lo = (sb(n, [P, KF, P], F32R, c) for n in ("hid_hi", "hid_lo"))
    y = [sb(f"y{j}", [P, D], F32, c) for j in range(2)]
    gathered = [sem(f"e_gathered{j}") for j in range(2)]
    scattered = [sem(f"e_scattered{j}") for j in range(2)]
    names = "e_made e_posb e_hot e_found_mm e_found e_src e_turn e_xhi e_xlo e_g e_u e_sig e_gated e_hid e_hturn " \
            "e_hhi e_hlo e_d e_y e_late e_dlo_v e_passed".split()
    (made, posb_done, hot_done, found_mm, found_done, src_done, turned, xhi_done, xlo_done, g_done, u_done, sig_done,
     gated, hid_done, hturned, hhi_done, hlo_done, d_done, y_done, late, dlo_v, passed) = (sem(n) for n in names)
    MADE = 5
    KH = KD // 2

    def turned_x():
        return ps[:, 4:6, 0:4 * CAP].rearrange("p a (k n) -> p a k n", n=CAP)

    def columns(ap):
        return ap[:, :, 0:CAP].rearrange("p (a k) n -> p a k n", a=2)

    def turned_h():
        return bank(k, 7, KF * CAP).rearrange("p (k n) -> p k n", n=CAP)

    with nc.Block() as block:
        @block.sync
        def _(sp):
            n = sp.value_load(halves[0:1, 1:2], min_val=EXPERTS, max_val=2 * MAX_HALVES)
            sp.wait_ge(dlo, 1)
            sp.wait_ge(dlo_v, 1)
            sp.dma_start(w_d[:], wd[1].rearrange("(k p) n -> p k n", p=P)).then_inc(d_in, 16)
            with sp.Fori(2, n) as b:
                e = sp.value_load(block_e[0:1, bass.ds(b, 1)], min_val=0, max_val=EXPERTS - 1)
                g, u, d = (w_[bass.ds(e, 1)].rearrange("o (k p) n -> p (o k) n", p=P) for w_ in (wg, wu, wd))
                sp.wait_ge(glo, 2 * b)
                sp.dma_start(w_g[:], g).then_inc(g_in, 16)
                sp.wait_ge(ulo, b)
                sp.dma_start(w_u[:], u).then_inc(u_in, 16)
                sp.wait_ge(dlo, b)
                sp.wait_ge(dlo_v, b)
                sp.dma_start(w_d[:], d).then_inc(d_in, 16)
            sp.wait_ge(glo, 2 * n)
            sp.dma_start(w_g[0:1, 0, :], wg[0, 0:1, :]).then_inc(g_in, 16)
            sp.wait_ge(ulo, n)
            sp.dma_start(w_u[0:1, 0, :], wu[0, 0:1, :]).then_inc(u_in, 16)

        @block.gpsimd
        def _(pool):
            pool.iota(place[:], [[1, CAP]], base=0, channel_multiplier=0,
                      allow_small_or_imprecise_dtypes=True).then_inc(made, 1)
            for j in range(2):
                G.step(pool.memset(x_g[j][:], 0.0))

            def gather(b, j, first=False):
                pool.wait_ge(src_done, b + 1)
                if not first:
                    pool.wait_ge(turned, b - 1)
                pool.sem_inc(passed, 1)
                pool.indirect_dma_start(x_g[j][0:CAP, :], None, k["h2_dram"][:, :],
                                        bass.IndirectOffsetOnAxis(ap=src[0:CAP, :], axis=0),
                                        bounds_check=T - 1, oob_is_err=False).then_inc(gathered[j], 16)

            def scatter(j):
                pool.indirect_dma_start(k["y2_dram"][:, :], bass.IndirectOffsetOnAxis(ap=dst[j][0:CAP, :], axis=0),
                                        y[j][0:CAP, :], None, bounds_check=2 * T - 1,
                                        oob_is_err=False).then_inc(scattered[j], 16)

            for j in range(2):
                gather(j, j, first=True)
            for j in range(2):
                G.step(pool.memset(dst[j][:], 2 * T))
                G.step(pool.memset(y[j][:], 0.0))
            for j in range(2):
                scatter(j)
            n2 = pool.value_load(halves[0:1, 0:1], min_val=EXPERTS // 2, max_val=MAX_HALVES)
            with pool.Fori(0, n2) as i:
                for j in range(2):
                    b = 2 * i + j
                    pool.wait_ge(dhi, b + 1)
                    pool.tensor_tensor(d_lo[:, 0:KF - 1], w_d[:, 0:KF - 1], d_hi[:, 0:KF - 1].bitcast(F32),
                                       ALU.subtract).then_inc(dlo, 1)
                    gather(b + 2, j)
                    pool.wait_ge(y_done, b + 3)
                    pool.wait_ge(late, 3 * b + 3)
                    pool.sem_inc(passed, 1)
                    scatter(j)
            for j in range(2):
                pool.wait_ge(scattered[j], 16 * n2 + 16)
                pool.wait_ge(gathered[j], 16 * n2 + 16)

        @block.scalar
        def _(act):
            def g_split(b):
                act.wait_ge(g_in, 16 * b + 16)
                for m in range(2):
                    act.activation(g_hi[:, m * KH:(m + 1) * KH], w_g[:, m * KH:(m + 1) * KH], ACT.Copy).then_inc(ghi, 1)

            def u_split(b):
                act.wait_ge(u_in, 16 * b + 16)
                act.activation(u_hi[:], w_u[:], ACT.Copy).then_inc(uhi, 1)

            def x_split(b):
                act.wait_ge(turned, b + 1)
                act.activation(columns(x_hi), turned_x(), ACT.Copy).then_inc(xhi_done, 1)

            act.wait_ge(made, MADE)
            x_split(0)
            n2 = act.value_load(halves[0:1, 0:1], min_val=EXPERTS // 2, max_val=MAX_HALVES)
            with act.Fori(0, n2) as i:
                for j in range(2):
                    b = 2 * i + j
                    act.wait_ge(d_in, 16 * b + 16)
                    act.wait_ge(d_done, b + 1)
                    act.activation(d_hi[:], w_d[:], ACT.Copy).then_inc(dhi, 1)
                    act.wait_ge(g_done, b + 1)
                    act.wait_ge(hid_done, b + 1)
                    act.activation(hid[0:CAP], bank(k, 0, FF, CAP), ACT.Sigmoid).then_inc(sig_done, 1)
                    g_split(b + 1)
                    act.wait_ge(u_done, b + 1)
                    x_split(b + 1)
                    act.wait_ge(hturned, b + 1)
                    act.activation(hid_hi[:, :, 0:CAP], turned_h(), ACT.Copy).then_inc(hhi_done, 1)
                    u_split(b + 1)
                    act.wait_ge(d_done, b + 2)
                    act.wait_ge(late, 3 * b + 3)
                    act.activation(y[j][0:CAP, :], ps[0:CAP, 2:4, :].rearrange("p b n -> p (b n)"), ACT.Copy,
                                   scale=gate[0:CAP, j, :]).then_inc(y_done, 1)

        @block.vector
        def _(dve):
            dve.sem_inc(hid_done, 1)
            dve.wait_ge(made, 1)

            def find(b, e):
                dve.wait_ge(found_mm, b + 1)
                dve.tensor_copy(pay_b[:], pay[:, :, bass.ds(e, 1), :].rearrange("p t o n -> p t (o n)"))\
                   .then_inc(posb_done, 1)
                dve.tensor_scalar(pos_b[:], pos[:, :, bass.ds(e, 1)].rearrange("p t o -> p (t o)"),
                                  block_j[:, bass.ds(b, 1)], None, ALU.add).then_inc(posb_done, 1)
                dve.wait_ge(posb_done, 2 * b + 2)
                for t in range(NT):
                    ins = dve.tensor_scalar(hot[:, t, :], place[:], pos_b[:, t:t + 1], None, ALU.is_equal)
                ins.then_inc(hot_done, 1)

            def found_out(b, j, before=None):
                dve.wait_ge(found_mm, b + 2)
                dve.tensor_copy(found[0:CAP, j, :], ps[0:CAP, 6, 0:4]).then_inc(found_done, 1)
                dve.wait_ge(found_done, 2 * b + 1)
                dve.tensor_scalar(far[0:CAP], found[0:CAP, j, 2:3], -FAR, FAR, ALU.mult, ALU.add).then_inc(found_done, 1)
                dve.wait_ge(found_done, 2 * b + 2)
                if before is not None:
                    dve.wait_ge(gathered[1 - j], before)
                dve.tensor_tensor(src[0:CAP], found[0:CAP, j, 0:1], far[0:CAP], ALU.add).then_inc(src_done, 1)
                dve.wait_ge(src_done, b + 1)

            def g_split(b, m):
                dve.wait_ge(ghi, 2 * b + m + 1)
                part = slice(m * KH, (m + 1) * KH)
                dve.tensor_tensor(g_lo[:, part], w_g[:, part], g_hi[:, part].bitcast(F32), ALU.subtract).then_inc(glo, 1)

            def u_split(b):
                dve.wait_ge(uhi, b + 1)
                dve.tensor_tensor(u_lo[:], w_u[:], u_hi[:].bitcast(F32), ALU.subtract).then_inc(ulo, 1)

            def x_split(b):
                dve.wait_ge(xhi_done, b + 1)
                dve.tensor_tensor(columns(x_lo), turned_x(), columns(x_hi).bitcast(F32), ALU.subtract).then_inc(xlo_done, 1)

            find(0, 0)
            found_out(0, 0)
            for half in (x_hi, x_lo, hid_hi, hid_lo):
                dve.memset(half[:].bitcast(F32), 0.0).then_inc(made, 1)
            find(1, 1)
            found_out(1, 1, before=16)
            dve.wait_ge(made, MADE)
            x_split(0)
            n2 = dve.value_load(halves[0:1, 0:1], min_val=EXPERTS // 2, max_val=MAX_HALVES)
            with dve.Fori(0, n2) as i:
                for j in range(2):
                    b = 2 * i + j
                    dve.wait_ge(y_done, b + 1)
                    dve.wait_ge(scattered[j], 16 * i + 16)
                    dve.tensor_copy(gate[0:CAP, j, :], found[0:CAP, j, 3:4]).then_inc(late, 1)
                    dve.tensor_scalar(late_far[0:CAP], found[0:CAP, j, 2:3], -FAR, FAR, ALU.mult, ALU.add).then_inc(late, 1)
                    dve.wait_ge(late, 3 * b + 2)
                    dve.tensor_tensor(dst[j][0:CAP], found[0:CAP, j, 1:2], late_far[0:CAP], ALU.add).then_inc(late, 1)
                    dve.wait_ge(late, 3 * b + 3)
                    e = dve.value_load(block_e[0:1, bass.ds(b + 2, 1)], min_val=0, max_val=EXPERTS - 1)
                    find(b + 2, e)
                    found_out(b + 2, j, before=16 * i + 16 + 16 * j)
                    dve.wait_ge(dhi, b + 1)
                    dve.tensor_tensor(d_lo[:, KF - 1], w_d[:, KF - 1], d_hi[:, KF - 1].bitcast(F32),
                                      ALU.subtract).then_inc(dlo_v, 1)
                    dve.wait_ge(sig_done, b + 1)
                    dve.tensor_tensor(hid[0:CAP], bank(k, 0, FF, CAP), hid[0:CAP], ALU.mult).then_inc(gated, 1)
                    g_split(b + 1, 0)
                    dve.wait_ge(u_done, b + 1)
                    dve.wait_ge(gated, b + 1)
                    dve.tensor_tensor(hid[0:CAP], bank(k, 1, FF, CAP), hid[0:CAP], ALU.mult).then_inc(hid_done, 1)
                    x_split(b + 1)
                    dve.wait_ge(hhi_done, b + 1)
                    dve.tensor_tensor(hid_lo[:, :, 0:CAP], turned_h(), hid_hi[:, :, 0:CAP].bitcast(F32), ALU.subtract)\
                       .then_inc(hlo_done, 1)
                    g_split(b + 1, 1)
                    u_split(b + 1)

        @block.tensor
        def _(pe):
            pe.sem_inc(found_mm, 1)
            pe.sem_inc(d_done, 1)
            pe.sem_inc(y_done, 2)

            def find(b, first=False):
                pe.wait_ge(hot_done, b + 1)
                if not first:
                    pe.wait_ge(found_done, 2 * b - 1)
                for t in range(NT):
                    mm = pe.matmul(ps[0:CAP, 6, 0:4], hot[:, t, :], pay_b[:, t, :], start=(t == 0), stop=(t == NT - 1))
                mm.then_inc(found_mm, 1)

            def turn_x(b, j, count):
                pe.wait_ge(gathered[j], count)
                if not (isinstance(b, int) and b == 0):
                    pe.wait_ge(xlo_done, b)
                for kd in range(KD):
                    mm = pe.transpose(ps[:, 4 + kd // 4, (kd % 4) * CAP:(kd % 4 + 1) * CAP],
                                      x_g[j][0:CAP, kd * P:(kd + 1) * P], ident[0:CAP, 0:CAP])
                mm.then_inc(turned, 1)

            def product(out, xs, ws, chunks, cols):
                n = 0
                for kd in range(chunks):
                    for x_, w_ in ((xs[0], ws[0]), (xs[1], ws[0]), (xs[0], ws[1])):
                        mm = pe.matmul(out, x_[:, kd, :], w_[:, kd, cols], start=(n == 0), stop=(n == 3 * chunks - 1))
                        n += 1
                return mm

            find(0, first=True)
            turn_x(0, 0, 16)
            find(1)
            n2 = pe.value_load(halves[0:1, 0:1], min_val=EXPERTS // 2, max_val=MAX_HALVES)
            with pe.Fori(0, n2) as i:
                for j in range(2):
                    b = 2 * i + j
                    pe.wait_ge(xlo_done, b + 1)
                    pe.wait_ge(glo, 2 * b + 2)
                    pe.wait_ge(hid_done, b + 1)
                    product(bank(k, 0), (x_hi, x_lo), (g_hi, g_lo), KD, slice(0, FF)).then_inc(g_done, 1)
                    find(b + 2)
                    pe.wait_ge(ulo, b + 1)
                    product(bank(k, 1), (x_hi, x_lo), (u_hi, u_lo), KD, slice(0, FF)).then_inc(u_done, 1)
                    turn_x(b + 1, 1 - j, 16 * i + 16 + 16 * j)
                    pe.wait_ge(hid_done, b + 2)
                    for f in range(KF):
                        mm = pe.transpose(ps[:, 7, f * CAP:(f + 1) * CAP], hid[0:CAP, f * P:(f + 1) * P],
                                          ident[0:CAP, 0:CAP])
                    mm.then_inc(hturned, 1)
                    pe.wait_ge(hlo_done, b + 1)
                    pe.wait_ge(dlo, b + 1)
                    pe.wait_ge(dlo_v, b + 1)
                    pe.wait_ge(y_done, b + 2)
                    for m in range(D // HALF):
                        mm = product(bank(k, 2 + m), (hid_hi, hid_lo), (d_hi, d_lo), KF, slice(m * HALF, (m + 1) * HALF))
                    mm.then_inc(d_done, 1)


def combine(k, c):
    nc, sb, sem, a = (k[n] for n in ("nc", "sb", "sem", "a"))
    x1 = sb("c_x1", [P, NT, D], F32, c)
    ya = sb("c_ya", [P, NT, D], F32, c)
    yb = sb("c_yb", [P, NT, D], F32, c)
    sq = sb("c_sq", [P, D], F32, c)
    gf = sb("gf", [P, D], F32, c)
    ss, rms, inv = (sb(n, [P, NT], F32, c) for n in ("c_ss", "c_rms", "c_inv"))
    loads = [sem(f"c_loads{t}") for t in range(NT)]
    small, sum1, sum2, ssd, rmsd, invd, od, stored = (
        sem(f"c_{n}") for n in ("small", "sum1", "sum2", "ss", "rms", "inv", "out", "stored"))
    with nc.Block() as block:
        @block.sync
        def _(sp):
            for t in range(NT):
                rows = slice(t * P, (t + 1) * P)
                sp.dma_start(ya[:, t], k["y2_dram"][rows, :]).then_inc(loads[t], 16)
                sp.dma_start(yb[:, t], k["y2_dram"][T + t * P:T + (t + 1) * P, :]).then_inc(loads[t], 16)
                sp.dma_start(x1[:, t], k["x1_dram"][rows, :]).then_inc(loads[t], 16)
                if t == 0:
                    sp.dma_start(gf[:], a["ln_f_g"].rearrange("(o n) -> o n", o=1).partition_broadcast(P)
                                 .rearrange("p o n -> p (o n)")).then_inc(small, 16)
            for t in range(NT):
                sp.wait_ge(od, t + 1)
                sp.dma_start(a["out"][0, t * P:(t + 1) * P, :], ya[:, t]).then_inc(stored, 16)
            sp.wait_ge(stored, 16 * NT)

        @block.vector
        def _(dve):
            for t in range(NT + 1):
                if t < NT:
                    dve.wait_ge(loads[t], 48)
                    dve.tensor_tensor(ya[:, t], ya[:, t], yb[:, t], ALU.add).then_inc(sum1, 1)
                    dve.wait_ge(sum1, t + 1)
                    dve.tensor_tensor(x1[:, t], x1[:, t], ya[:, t], ALU.add).then_inc(sum2, 1)
                if t == 1:
                    dve.wait_ge(small, 16)
                if t >= 1:
                    u = t - 1
                    dve.wait_ge(rmsd, t)
                    dve.reciprocal(inv[:, u:u + 1], rms[:, u:u + 1]).then_inc(invd, 1)
                    dve.wait_ge(invd, t)
                    dve.wait_ge(sum2, t)
                    dve.scalar_tensor_tensor(ya[:, u], x1[:, u], inv[:, u:u + 1], gf[:], ALU.mult, ALU.mult).then_inc(od, 1)

        @block.scalar
        def _(act):
            for t in range(NT):
                act.wait_ge(sum2, t + 1)
                if t >= 1:
                    act.wait_ge(ssd, t)
                act.activation(sq[:], x1[:, t], ACT.Square, accum_out=ss[:, t:t + 1]).then_inc(ssd, 1)
                act.wait_ge(ssd, t + 1)
                act.activation(rms[:, t:t + 1], ss[:, t:t + 1], ACT.Sqrt, bias=k["eps_t"][:], scale=1.0 / D).then_inc(rmsd, 1)


def kernel(**inputs):
    import concourse.bacc as bacc
    from concourse.bass_utils import run_bass_kernel_spmd

    nc = bacc.Bacc("TRN2", target_bir_lowering=False, num_devices=1)
    arrays, args = {}, {}
    for name, value in inputs.items():
        arr = np.ascontiguousarray(value)
        arrays[name] = arr
        args[name] = nc.dram_tensor(name, arr.shape, mybir.dt.from_np(arr.dtype), kind="ExternalInput").ap()
    args["out"] = nc.dram_tensor("out", (1, T, D), F32, kind="ExternalOutput").ap()
    build(nc, args)
    r = run_bass_kernel_spmd(nc, [arrays], core_ids=[0])
    return r.results[0]["out"]
```
